# Optimizing a Trainium2 kernel written in Bass

```python
import jax, jax.numpy as jnp
from jax import lax
import numpy as np

D_MODEL = 1024
BATCH = 1
SEQ = 2048
DEPTH = 1
DEC_BATCH = 8
DEC_SEQ = 4
PAST_LEN = 16384
PAGE_SIZE = 128

W_A = D_MODEL // 2
HGRN_EXPAND = 128
H_A = W_A // HGRN_EXPAND
DK = HGRN_EXPAND
DV = W_A // H_A
CHUNK = 32
W_B = D_MODEL // 2
POOL_WINDOWS = (2, 4, 8, 16)
N_POOL_GROUPS = len(POOL_WINDOWS)
G_B = W_B // N_POOL_GROUPS
POOL_BUF = max(POOL_WINDOWS) - 1
D_IN = 4 * W_A + 2 * W_B + 2 * D_MODEL
EPS = 1e-6

kernel_name = 'hgrn2_pool_gated_hybrid_step'

def _rmsnorm(x, g):
    x32 = x.astype(jnp.float32)
    y = x32 * lax.rsqrt(jnp.mean(x32 * x32, axis=-1, keepdims=True) + EPS)
    return (y * g.astype(jnp.float32)).astype(x.dtype)

def _hgrn2_chunked(q, k, v, logf, s0):
    B, T, H, _ = q.shape
    C = CHUNK if T >= CHUNK else T
    n = -(-T // C)
    pad = n * C - T

    def to_chunks(a):
        a = jnp.pad(a, ((0, 0), (0, pad), (0, 0), (0, 0)))
        return a.reshape(B, n, C, H, a.shape[-1]).transpose(1, 0, 3, 2, 4)

    qc, kc, vc, gc = to_chunks(q), to_chunks(k), to_chunks(v), to_chunks(logf)
    causal = jnp.tril(jnp.ones((C, C), dtype=bool))

    def step(S, blk):
        qb, kb, vb, gb = blk
        b = jnp.cumsum(gb, axis=2)
        ref = b[:, :, C // 2:C // 2 + 1]
        b_last = b[:, :, C - 1:C]
        scores = jnp.einsum('bhtd,bhsd->bhts', qb * jnp.exp(b - ref), kb * jnp.exp(ref - b))
        scores = jnp.where(causal, scores, 0.0)
        o = (jnp.einsum('bhts,bhsv->bhtv', scores, vb)
             + jnp.einsum('bhtd,bhdv->bhtv', qb * jnp.exp(b), S))
        S = (jnp.exp(b_last[:, :, 0])[..., None] * S
             + jnp.einsum('bhsd,bhsv->bhdv', kb * jnp.exp(b_last - b), vb))
        return S, o

    S, o = lax.scan(step, s0, (qc, kc, vc, gc))
    o = o.transpose(1, 0, 3, 2, 4).reshape(B, n * C, H, -1)[:, :T]
    return o, S

def _multiscale_pool(u, buf, pos0):
    B, T, _ = u.shape
    u32 = u.astype(jnp.float32)
    ext = jnp.concatenate([buf.astype(jnp.float32), u32], axis=1)
    cs = jnp.concatenate([jnp.zeros((B, 1, W_B), jnp.float32), jnp.cumsum(ext, axis=1)], axis=1)
    pos = pos0 + jnp.arange(T)
    outs = []
    for gi, w in enumerate(POOL_WINDOWS):
        lo, hi = gi * G_B, (gi + 1) * G_B
        s = cs[:, POOL_BUF + 1:POOL_BUF + 1 + T, lo:hi] - cs[:, POOL_BUF + 1 - w:POOL_BUF + 1 - w + T, lo:hi]
        cnt = jnp.minimum(pos + 1, w).astype(jnp.float32)
        outs.append(s / cnt[None, :, None])
    return jnp.concatenate(outs, axis=-1) - u32

def _layer(x, s0, buf0, pos0, lb, norm_g, w_in, hgrn_norm_g, w_proj_a, w_pool, pool_scale, w_proj_b, w_out):
    B, T, _ = x.shape
    dt = x.dtype
    h = _rmsnorm(x, norm_g)
    z = h @ w_in
    q, f, i, g_a, u, g_b, m_a, m_b = jnp.split(
        z, np.cumsum([W_A, W_A, W_A, W_A, W_B, W_B, D_MODEL]).tolist(), axis=-1)
    fgate = lb + (1.0 - lb) * jax.nn.sigmoid(f.astype(jnp.float32))
    logf = jnp.log(fgate)
    kin = 1.0 - fgate
    qf = jax.nn.silu(q.astype(jnp.float32)) * (DK ** -0.5)
    hd = lambda a: a.reshape(B, T, H_A, -1)
    o, s_new = _hgrn2_chunked(hd(qf), hd(kin), hd(i.astype(jnp.float32)), hd(logf), s0)
    o = _rmsnorm(o, hgrn_norm_g) * jax.nn.silu(hd(g_a.astype(jnp.float32)))
    y_a = o.reshape(B, T, W_A).astype(dt) @ w_proj_a
    pooled = _multiscale_pool(u, buf0, pos0).reshape(B, T, N_POOL_GROUPS, G_B)
    mixed = jnp.einsum('btgc,gcd->btgd', pooled, w_pool.astype(jnp.float32)).reshape(B, T, W_B)
    yb = mixed * pool_scale.astype(jnp.float32) * jax.nn.silu(g_b.astype(jnp.float32))
    y_b = yb.astype(dt) @ w_proj_b
    merged = jax.nn.sigmoid(m_a) * y_a + jax.nn.sigmoid(m_b) * y_b
    out = x + merged @ w_out
    new_buf = jnp.concatenate([buf0.astype(dt), u], axis=1)[:, -POOL_BUF:]
    return out, s_new, new_buf

def setup_inputs(seed: int = 0) -> dict:
    key = jax.random.key(seed)
    ks = jax.random.split(key, 14)
    nrm = lambda k, s: jax.random.normal(k, s, jnp.float32)
    return {
        'x_prompt': nrm(ks[0], (BATCH, SEQ, D_MODEL)),
        'x_sample': nrm(ks[1], (DEC_BATCH, DEC_SEQ, D_MODEL)),
        'state_hgrn': 0.5 * nrm(ks[2], (DEPTH, DEC_BATCH, H_A, DK, DV)),
        'state_pool': nrm(ks[3], (DEPTH, DEC_BATCH, POOL_BUF, W_B)),
        'norm_g': 1.0 + 0.02 * nrm(ks[4], (DEPTH, D_MODEL)),
        'w_in': nrm(ks[5], (DEPTH, D_MODEL, D_IN)) * D_MODEL ** -0.5,
        'lb_logits': 0.1 * nrm(ks[6], (DEPTH + 1, W_A)),
        'hgrn_norm_g': 1.0 + 0.02 * nrm(ks[7], (DEPTH, DV)),
        'w_proj_a': nrm(ks[8], (DEPTH, W_A, D_MODEL)) * W_A ** -0.5,
        'w_pool': nrm(ks[9], (DEPTH, N_POOL_GROUPS, G_B, G_B)) * G_B ** -0.5,
        'pool_scale': 1.0 + 0.1 * nrm(ks[10], (DEPTH, W_B)),
        'w_proj_b': nrm(ks[11], (DEPTH, W_B, D_MODEL)) * W_B ** -0.5,
        'w_out': nrm(ks[12], (DEPTH, D_MODEL, D_MODEL)) * D_MODEL ** -0.5,
        'final_norm_g': 1.0 + 0.02 * nrm(ks[13], (D_MODEL,)),
    }

def reference(x_prompt, x_sample, state_hgrn, state_pool, norm_g, w_in, lb_logits, hgrn_norm_g,
              w_proj_a, w_pool, pool_scale, w_proj_b, w_out, final_norm_g):
    lbs = jnp.cumsum(jax.nn.softmax(lb_logits.astype(jnp.float32), axis=0), axis=0)
    yp, ys = x_prompt, x_sample
    hp, pp, hs, ps = [], [], [], []
    for l in range(DEPTH):
        s0p = jnp.zeros((BATCH, H_A, DK, DV), jnp.float32)
        b0p = jnp.zeros((BATCH, POOL_BUF, W_B), x_prompt.dtype)
        yp, s_p, b_p = _layer(yp, s0p, b0p, 0, lbs[l], norm_g[l], w_in[l], hgrn_norm_g[l],
                              w_proj_a[l], w_pool[l], pool_scale[l], w_proj_b[l], w_out[l])
        ys, s_s, b_s = _layer(ys, state_hgrn[l].astype(jnp.float32), state_pool[l], PAST_LEN, lbs[l],
                              norm_g[l], w_in[l], hgrn_norm_g[l], w_proj_a[l], w_pool[l],
                              pool_scale[l], w_proj_b[l], w_out[l])
        hp.append(s_p.astype(state_hgrn.dtype)); pp.append(b_p.astype(state_pool.dtype))
        hs.append(s_s.astype(state_hgrn.dtype)); ps.append(b_s.astype(state_pool.dtype))
    y_prompt = _rmsnorm(yp, final_norm_g)
    y_sample = _rmsnorm(ys, final_norm_g)
    return (y_prompt, y_sample, jnp.stack(hp), jnp.stack(pp), jnp.stack(hs), jnp.stack(ps))


_drawn_inputs = setup_inputs


def setup_inputs(seed=0):
    import zlib

    import numpy as np

    out = dict(_drawn_inputs(seed))
    spreads = {}
    factors = {}
    for name, (base, spread) in spreads.items():
        noise = np.random.default_rng([zlib.crc32(name.encode()), seed]).standard_normal(out[name].shape)
        drawn = base * np.exp(spread * noise) if base else spread * noise
        out[name] = __import__('jax').numpy.asarray(drawn.astype(out[name].dtype))
    for name, factor in factors.items():
        out[name] = (out[name] * factor).astype(out[name].dtype)
    return out
```

```python
from contextlib import ExitStack

import numpy as np

import concourse.bass as bass
from concourse import mybir

F32 = mybir.dt.float32
F32R = mybir.dt.float32r
U32 = mybir.dt.uint32
ALU = mybir.AluOpType
ACT = mybir.ActivationFunctionType

P = 128
D = 1024
KD = D // P
SEQ = 2048
NB, NT = 8, 4
SAMPLE = NB * NT
T = 416
TILES = (SEQ + SAMPLE) // T
H = 4
G = 4
CHUNK = 32
NC = T // CHUNK
PT = T - SAMPLE
BUF = 15
WINDOWS = (2, 4, 8, 16)
EPS = 1e-6
QSCALE = float(P) ** -0.5
RAW = 2
RING = 4
AHEAD = RING - 1

UNITS = [(kind, h) for h in range(H) for kind in "fqig"]
UNITS += [(kind, g) for g in range(G) for kind in "ub"]
UNITS += [("ma", 0), ("mb", 0)]
for _j in range(1, KD):
    UNITS += [("ma", _j), ("mb", _j), ("y", _j - 1)]
UNITS += [("y", KD - 1)]
UNITS += [("out", _j) for _j in range(KD)]
NU = len(UNITS)
SLOT = {u: s for s, u in enumerate(UNITS)}

ACCS = []
for _kind, _i in UNITS:
    ACCS += [("ya", _i), ("yb", _i)] if _kind == "y" else [(_kind, _i)]
NA = len(ACCS)
ACC = {a: n for n, a in enumerate(ACCS)}
NZ = 4
LAST_ACC = [ACC[("yb", i)] if kind == "y" else ACC[(kind, i)] for kind, i in UNITS]

MIX_SLOT = {22: 0, 23: 1, 25: 2, 26: 3}
XSQ_SLOT = {28 + 2 * k: k for k in range(KD)}
XNORM = 46
H_SLOT = {47 + k: k for k in range(KD)}

B4_USES, B5_USES = [], []
for _s in range(NU):
    for _h in range(H):
        if _s == 4 * _h + 12:
            B4_USES.append(("ssq", _h))
        if _s == 4 * _h + 6:
            B4_USES.append(("tk", _h))
            B5_USES.append(("tv", _h))
        if _s == 4 * _h + 7:
            B4_USES.append(("scores", _h))
        if _s == 4 * _h + 9:
            B5_USES.append(("o", _h))
    if _s == XNORM:
        B4_USES.append(("xssq", 0))
B5_USES.append(("yssq", 0))

C_NG, C_GN, C_PS, C_FG, C_LB = 0, 8, 9, 13, 21
C_N = 29

Y_ORDER = [k for _, k in sorted([(4 * h + 13, h) for h in range(H)]
                                + [(s + 0.5, 4 + g) for s, g in MIX_SLOT.items()])]
MASKS = 21
ZEROED = 6
LB_STEPS = 8
RC_FIRST = G + 1


def step_kernel(nc, xT, w_all, consts, w_pool, s_in, buf_in, yT, sp_out, pp_out, ss_out, ps_out):
    with ExitStack() as ctx:
        start = (int(nc.sbuf_base) + 63) // 64 * 64
        top = [start]

        def put(name, shape, dt=F32, at=None, parts=P):
            size = 4 * int(np.prod(shape))
            if at is None:
                at = top[0]
                top[0] += (size + 31) // 32 * 32
            return nc.alloc_sbuf_tensor_at(name, [parts, *shape], dt, offset=at)

        def region(size):
            at = top[0]
            top[0] += (size + 31) // 32 * 32
            return at

        B = 4 * T
        wraw = [put(f"wraw{i}", [D]) for i in range(RAW)]
        whi = [put(f"whi{i}", [D], F32R) for i in range(RING)]
        wlo = [put(f"wlo{i}", [D], F32R) for i in range(RING)]
        hhi = [put(f"hhi{k}", [T], F32R) for k in range(KD)]
        hlo = [put(f"hlo{k}", [T], F32R) for k in range(KD)]
        yhi = [put(f"yhi{k}", [T], F32R) for k in range(KD)]
        ylo = [put(f"ylo{k}", [T], F32R) for k in range(KD)]
        r1 = region(16 * B)
        mhi = [put(f"mhi{k}", [T], F32R, r1 + k * B) for k in range(KD)]
        mlo = [put(f"mlo{k}", [T], F32R, r1 + (KD + k) * B) for k in range(KD)]
        r2 = region(KD * B)
        xin = put("xin", [KD, T], F32, r2)
        own = region(2 * B)
        hg = [r1 + i * B for i in range(16)] + [r2 + i * B for i in range(8)] + [own, own + B]
        names = ["b", "d", "dl", "e1", "e2", "e4", "e30", "e31", "q20", "q21", "ga0", "ga1", "ga2", "os",
                 "osq", "rst", "og0", "og1", "sf0", "sf1", "qf0", "qf1", "kin0", "kin1", "vt", "logf"]
        buf = {n: put("h_" + n, [T], F32, at) for n, at in zip(names, hg)}
        sf = [buf["sf0"], buf["sf1"]]
        qf = [buf["qf0"], buf["qf1"]]
        kin = [buf["kin0"], buf["kin1"]]
        ga = [buf["ga0"], buf["ga1"], buf["ga2"]]
        e3 = [buf["e30"], buf["e31"]]
        q2 = [buf["q20"], buf["q21"]]
        og = [buf["og0"], buf["og1"]]
        vt, logf, bc, dd, dl = buf["vt"], buf["logf"], buf["b"], buf["d"], buf["dl"]
        e1, e2, e4 = buf["e1"], buf["e2"], buf["e4"]
        o_sb, osq, rst = buf["os"], buf["osq"], buf["rst"]
        r3 = region(10 * B + 128)
        gA = [put(f"gA{i}", [T], F32, r3 + a * B) for i, a in enumerate((0, 2, 4))]
        gB = [put(f"gB{i}", [T], F32, r3 + a * B) for i, a in enumerate((1, 3, 5))]
        mA = [put(f"mA{i}", [T], F32, r3 + (6 + i) * B) for i in range(2)]
        mB = [put(f"mB{i}", [T], F32, r3 + (8 + i) * B) for i in range(2)]
        s_all = put("s_all", [NC, P], F32, r3)
        bg_own = region(B)
        bg = [put("bg0", [T], F32, bg_own), put("bg1", [T], F32, r3 + 4 * B), put("bg2", [T], F32, r3 + 5 * B)]
        pa = put("pa", [BUF + T], F32, r3 + 6 * B)
        pb = put("pb", [BUF + T], F32, r3 + 6 * B + 1728)
        pooled = [put(f"pooled{i}", [T], F32, r3 + 6 * B + 3456 + i * B) for i in range(2)]
        h32 = [put(f"h32_{i}", [T], F32, r3 + (4 + i) * B) for i in range(2)]
        ysq = [put(f"ysq{i}", [T], F32, r3 + i * B) for i in range(2)]
        yacc = put("yacc", [T], F32, r3 + 6 * B)
        yrs = put("yrs", [T], F32, r3 + 8 * B)
        xsq = [put(f"xsq{i}", [T]) for i in range(2)]
        xacc = put("xacc", [T])
        xrs = xsq[0]
        xr_at = region(KD * B)
        xres = put("xres", [KD, T], F32, xr_at)
        s0 = [put(f"s0_{i}", [NB, P], F32, xr_at + 4096 * i) for i in range(2)]
        snew = put("snew", [NB, P], F32, xr_at + 8192)
        ktm = put("ktm", [4, P])
        vtm = put("vtm", [4, P])
        vbd = put("vbd", [4, 4, P])
        vms = put("vms", [4, P])
        at_sb = put("at_sb", [T])
        ats = put("ats", [SAMPLE])
        carry = put("carry", [H, P])
        EXT = BUF + T
        ext = put("ext", [G, EXT])
        exts = put("exts", [G, NB, BUF + NT])
        pas = put("pas", [NB, BUF + NT])
        pbs = put("pbs", [NB, BUF + NT])
        wpl = put("wpl", [G, P])
        cst = put("cst", [C_N])
        smask = put("smask", [T])
        smask_s = put("smask_s", [SAMPLE])
        cmask = put("cmask", [3, 4, CHUNK])
        cmask_s = put("cmask_s", [NB, NT])
        bmask = put("bmask", [NB])
        ones = put("ones", [P])
        ident = put("ident", [P])
        lb = put("lb", [8, H])
        eps_t = put("eps_t", [1])
        rc = put("rc", [G, BUF])
        ptmp = put("ptmp", [BUF])
        assert top[0] <= nc.sbuf_usable_end, (top[0], nc.sbuf_usable_end)
        lb0, oml, noml = lb[:, 0], lb[:, 1], lb[:, 2]

        Z = [ctx.enter_context(nc.psum_tensor(f"Z{i}", [P, 512], F32)) for i in range(NZ)]
        B4, B5, B6, B7 = [ctx.enter_context(nc.psum_tensor(f"B{i}", [P, 512], F32)) for i in range(4, 8)]

        def sem(name):
            return ctx.enter_context(nc.semaphore(name))

        w_landed = [sem(f"w_landed{i}") for i in range(RAW)]
        xin_landed, xres_landed, cst_landed = sem("xin_landed"), sem("xres_landed"), sem("cst_landed")
        s0_landed, buf_landed = [sem(f"s0_landed{i}") for i in range(2)], sem("buf_landed")
        y_stored, snew_stored, ends_stored = sem("y_stored"), sem("snew_stored"), sem("ends_stored")
        acc_done, tv_done, tk_done, sc_done = sem("acc_done"), sem("tv_done"), sem("tk_done"), sem("sc_done")
        p_done, o_done, ssq_done, mix_done = sem("p_done"), sem("o_done"), sem("ssq_done"), sem("mix_done")
        xssq_done, yssq_done = sem("xssq_done"), sem("yssq_done")
        whi_made, sq_made, sg_made, sb_made = sem("whi_made"), sem("sq_made"), sem("sg_made"), sem("sb_made")
        logf_made, exp_made, osq_made, rst_made = sem("logf_made"), sem("exp_made"), sem("osq_made"), sem("rst_made")
        xsq_made, xrs_made, hhi_made = sem("xsq_made"), sem("xrs_made"), sem("hhi_made")
        yhi_made, mhi_made, ysq_made, yrs_made = sem("yhi_made"), sem("mhi_made"), sem("ysq_made"), sem("yrs_made")
        yln_made, lbe_made = sem("yln_made"), sem("lbe_made")
        wlo_made, kin_made, b_made, d_made = sem("wlo_made"), sem("kin_made"), sem("b_made"), sem("d_made")
        q_made, s_made, s0_copied, og_made = sem("q_made"), sem("s_made"), sem("s0_copied"), sem("og_made")
        t1_made, ylo_made, rc_used, pooled_made = sem("t1_made"), sem("ylo_made"), sem("rc_used"), sem("pooled_made")
        hist_kept, ybm_made, mul_made, mlo_made = sem("hist_kept"), sem("ybm_made"), sem("mul_made"), sem("mlo_made")
        h32_made, hlo_made, y_made, vms_made = sem("h32_made"), sem("hlo_made"), sem("y_made"), sem("vms_made")
        lb_made, zeroed, ptmp_made = sem("lb_made"), sem("zeroed"), sem("ptmp_made")
        vbd_made = sem("vbd_made")
        k_made, win_made, merged = sem("k_made"), sem("win_made"), sem("merged")
        xacc_made, yacc_made, masks = sem("xacc_made"), sem("yacc_made"), sem("masks")
        z_read = [sem(f"z_read{i}") for i in range(NZ)]
        b4_read, b5_read = sem("b4_read"), sem("b5_read")

        def nth(t, per, i):
            return t * per + (i + 1)

        def acc_ready(t, kind, i):
            return nth(t, NA, ACC[(kind, i)])

        def z_bank(kind, i):
            return Z[ACC[(kind, i)] % NZ]

        def z_sem(kind, i):
            return z_read[ACC[(kind, i)] % NZ]

        def z_done(t, kind, i):
            return nth(t, NA // NZ, ACC[(kind, i)] // NZ)

        def b4_done(t, use, h):
            return nth(t, len(B4_USES), B4_USES.index((use, h))) + 1

        def b5_done(t, use, h):
            return nth(t, len(B5_USES), B5_USES.index((use, h)))

        def landed(t, n):
            return 16 * (t * (NU // RAW) + n // RAW + 1)

        def s_value(t, last, h, i):
            per = 20 if last else NC
            return t * (H * NC) + h * per + i + 1

        def win_value(t, last, g, level, sample=False):
            before = sum(range(1, g + 1)) * (2 if last else 1)
            return t * 10 + before + (2 * level + sample if last else level) + 1

        def pooled_value(t, last, g):
            return t * G + g + 1

        block = ctx.enter_context(nc.Block())

        @block.sync
        def _(sp):
            sp.dma_start(xin[:], xT[0]).then_inc(xin_landed, 16)
            sp.dma_start(cst[:], consts).then_inc(cst_landed, 16)
            for n in range(RAW):
                sp.dma_start(wraw[n][:], w_all[n]).then_inc(w_landed[n], 16)
            sp.dma_start(wpl[:], w_pool).then_inc(cst_landed, 16)
            sp.dma_start(exts[:, :, :, 0:BUF], buf_in).then_inc(buf_landed, 16)

            def tile(t, last):
                for s in range(NU):
                    if s == 3 and last:
                        sp.wait_ge(y_stored, 16 * (TILES - 1))
                        for h in range(2):
                            sp.dma_start(s0[h][:], s_in[h]).then_inc(s0_landed[h], 16)
                    n = s + RAW
                    if n < NU or not last:
                        sp.wait_ge(wlo_made, nth(t, NU, s))
                        sp.dma_start(wraw[n % RAW][:], w_all[n % NU]).then_inc(w_landed[n % RAW], 16)
                    if s == 29 and not last:
                        sp.wait_ge(ylo_made, nth(t, 8, 7))
                        sp.dma_start(xin[:], xT[t + 1]).then_inc(xin_landed, 16)
                    if last and s in (13, 17, 21, 25):
                        h = (s - 13) // 4
                        sp.wait_ge(s_made, s_value(t, last, h, 19))
                        sp.dma_start(ss_out[h], snew[:]).then_inc(snew_stored, 16)
                        if h < 2:
                            sp.wait_ge(o_done, nth(t, H, h))
                            sp.dma_start(s0[h][:], s_in[h + 2]).then_inc(s0_landed[h], 16)
                    if s == 32:
                        if last:
                            sp.wait_ge(snew_stored, 16 * H)
                        else:
                            sp.wait_ge(y_stored, t * 16)
                        sp.dma_start(xres[:], xT[t]).then_inc(xres_landed, 16)
                if last:
                    sp.dma_start(sp_out, carry[:]).then_inc(ends_stored, 16)
                    sp.wait_ge(ybm_made, nth(t, G, G - 1))
                    sp.dma_start(pp_out, ext[:, :, PT:PT + BUF]).then_inc(ends_stored, 16)
                    sp.dma_start(ps_out, exts[:, :, :, NT:NT + BUF]).then_inc(ends_stored, 16)
                    sp.wait_ge(ends_stored, 48)
                    sp.wait_ge(snew_stored, 16 * H)
                    sp.wait_ge(y_stored, 16 * TILES)

            tile(0, False)
            with sp.Fori(1, TILES - 1) as t:
                tile(t, False)
            tile(TILES - 1, True)

        @block.tensor
        def _(pe):
            def three(out, parts, k_rhs, first, final):
                (wh, wl), (xh, xl) = parts, k_rhs
                pe.matmul(out, wh, xh, start=first, stop=False)
                pe.matmul(out, wh, xl, start=False, stop=False)
                return pe.matmul(out, wl, xh, start=False, stop=final)

            def xnorm_sum(value):
                pe.wait_ge(xacc_made, value * (KD - 1))
                pe.matmul(B4[:, 0:T], ones[:], xacc[:], start=True, stop=True).then_inc(xssq_done, 1)

            def small(t, last, s):
                for h in range(H):
                    base = 4 * h
                    if s == base + 12:
                        pe.wait_ge(osq_made, nth(t, H, h))
                        pe.wait_ge(b4_read, b4_done(t, "ssq", h) - 1)
                        pe.matmul(B4[:, 0:T], ones[:], osq[:], start=True, stop=True).then_inc(ssq_done, 1)
                    if s == base + 6:
                        pe.wait_ge(z_sem("i", h), z_done(t, "i", h))
                        pe.wait_ge(b5_read, b5_done(t, "tv", h) - 1)
                        transposes(B5, vt, tv_done)
                        pe.wait_ge(k_made, nth(t, 2 * H, 2 * h + 1))
                        pe.wait_ge(b4_read, b4_done(t, "tk", h) - 1)
                        transposes(B4, e4, tk_done)
                    if s == base + 7:
                        pe.wait_ge(q_made, nth(t, 2 * H, 2 * h + 1))
                        pe.wait_ge(b4_read, b4_done(t, "scores", h) - 1)
                        for g in range(3):
                            c = slice(g * P, (g + 1) * P)
                            pe.matmul(B4[:, c], e2[:, c], e1[:, c], start=True, stop=True)
                        pe.matmul(B4[0:SAMPLE, PT:T], e2[:, PT:T], e1[:, PT:T], start=True,
                                  stop=True).then_inc(sc_done, 1)
                        pe.wait_ge(vbd_made, nth(t, 4 * H, 4 * h + 3))
                        for g in range(2):
                            if h:
                                i = ((19, 15) if last else (11, 12))[g]
                                pe.wait_ge(s_made, s_value(t, last, h - 1, i))
                            else:
                                pe.wait_ge(ybm_made, t * G)
                            group(g, (B6, B7)[g])
                    if s == base + 8:
                        pe.wait_ge(s_made, s_value(t, last, h, 3))
                        group(2, B6)
                        pe.wait_ge(s_made, s_value(t, last, h, 7))
                        if last:
                            pe.wait_ge(vms_made, 2 * h + 1)
                            pe.matmul(B7[:], ktm[0:SAMPLE, 3, :], vbd[0:SAMPLE, 3], start=True,
                                      stop=True).then_inc(p_done, 1)
                        else:
                            pe.matmul(B7[:, 0:P], ktm[0:CHUNK, 3, :], vbd[0:CHUNK, 3, 0, :], start=True,
                                      stop=True).then_inc(p_done, 1)
                    if s == base + 9:
                        if last:
                            pe.wait_ge(s_made, s_value(t, last, h, 11))
                            pe.wait_ge(vms_made, 2 * h + 2)
                            pe.matmul(B6[:], ktm[0:SAMPLE, 3, :], vms[0:SAMPLE], start=True,
                                      stop=True).then_inc(p_done, 1)
                        outputs(t, last, h)
                if s in MIX_SLOT:
                    g = MIX_SLOT[s]
                    pe.wait_ge(pooled_made, pooled_value(t, last, g))
                    if g < 2:
                        pe.wait_ge(s_made, s_value(t, last, H - 1, 19 if last else NC - 1))
                    else:
                        pe.wait_ge(ybm_made, nth(t, G, g - 2))
                    pe.matmul((B6, B7)[g % 2][:, 0:T], wpl[:, g, :], pooled[g % 2][:], start=True,
                              stop=True).then_inc(mix_done, 1)
                if s == XNORM and not last:
                    pe.wait_ge(b4_read, b4_done(t, "xssq", 0) - 1)
                    xnorm_sum(t + 2)

            def transposes(bank, src, done):
                for g in range(3):
                    pe.transpose(bank[:, g * P:(g + 1) * P], src[:, g * P:(g + 1) * P], ident[:])
                pe.transpose(bank[0:SAMPLE, 3 * P:4 * P], src[:, PT:T], ident[:]).then_inc(done, 1)

            def group(g, bank):
                pe.matmul(bank[:], ktm[:, g, :], vbd[:, g], start=True, stop=True).then_inc(p_done, 1)

            def outputs(t, last, h):
                pe.wait_ge(b4_read, b4_done(t, "scores", h))
                pe.wait_ge(b5_read, b5_done(t, "o", h) - 1)
                for g in range(3):
                    c = slice(g * P, (g + 1) * P)
                    pe.matmul(B5[:, c], vtm[:, g, :], at_sb[:, c], start=(g == 0), stop=False,
                              skip_group_check=True)
                a3 = ats[0:SAMPLE, :] if last else at_sb[0:SAMPLE, PT:T]
                pe.matmul(B5[:, PT:T], vtm[0:SAMPLE, 3, :], a3, start=False, stop=False,
                          skip_group_check=True)
                pe.wait_ge(s_made, s_value(t, last, h, 11 if last else 12))
                pe.wait_ge(s0_copied, nth(t, H, h))
                for c in range(12 if last else NC):
                    mm = pe.matmul(B5[:, c * CHUNK:(c + 1) * CHUNK], s_all[:, c, :],
                                   q2[h % 2][:, c * CHUNK:(c + 1) * CHUNK], start=False,
                                   stop=(c == NC - 1), skip_group_check=True)
                if last:
                    pe.wait_ge(s0_landed[h % 2], 16 * (h // 2 + 1))
                    for b in range(NB):
                        c = PT + b * NT
                        mm = pe.matmul(B5[:, c:c + NT], s0[h % 2][:, b, :], q2[h % 2][:, c:c + NT],
                                       start=False, stop=(b == NB - 1), skip_group_check=True)
                mm.then_inc(o_done, 1)

            def product(t, s, acc, blocks):
                n = ACC[acc]
                pe.wait_ge(z_read[n % NZ], t * (NA // NZ) + n // NZ)
                out = Z[n % NZ][:, 0:T]
                for i, (k, hi, lo, ready, value) in enumerate(blocks):
                    if ready is not None:
                        pe.wait_ge(ready, value)
                    c = slice(k * P, (k + 1) * P)
                    mm = three(out, (whi[s % RING][:, c], wlo[s % RING][:, c]), (hi[:], lo[:]), i == 0,
                               i == len(blocks) - 1)
                mm.then_inc(acc_done, 1)

            def tile(t, last):
                for s, (kind, i) in enumerate(UNITS):
                    small(t, last, s)
                    pe.wait_ge(wlo_made, nth(t, NU, s))
                    if kind == "y":
                        def ready(k):
                            return (ylo_made, nth(t, 8, Y_ORDER.index(k))) if i == 0 else (None, None)
                        product(t, s, ("ya", i), [(k, yhi[k], ylo[k], *ready(k)) for k in range(4)])
                        product(t, s, ("yb", i), [(k, yhi[k], ylo[k], *ready(k)) for k in range(4, 8)])
                    elif kind == "out":
                        product(t, s, (kind, i), [
                            (k, mhi[k], mlo[k], *((mlo_made, nth(t, KD, k)) if i == 0 else (None, None)))
                            for k in range(KD)])
                    else:
                        product(t, s, (kind, i), [
                            (k, hhi[k], hlo[k], *((hlo_made, nth(t, KD, k)) if s == 0 else (None, None)))
                            for k in range(KD)])
                pe.wait_ge(yacc_made, nth(t, KD - 1, KD - 2))
                pe.wait_ge(b5_read, b5_done(t, "yssq", 0) - 1)
                pe.matmul(B5[:, 0:T], ones[:], yacc[:], start=True, stop=True).then_inc(yssq_done, 1)

            pe.wait_ge(masks, MASKS)
            pe.wait_ge(zeroed, ZEROED)
            pe.wait_ge(cst_landed, 32)
            xnorm_sum(1)
            tile(0, False)
            with pe.Fori(1, TILES - 1) as t:
                tile(t, False)
            tile(TILES - 1, True)

        @block.scalar
        def _(act):
            def split(t, s_or_n):
                n = s_or_n
                act.wait_ge(w_landed[n % RAW], landed(t, n))
                act.activation(whi[n % RING][:], wraw[n % RAW][:], ACT.Copy).then_inc(whi_made, 1)

            def x_square(value, k):
                if k == 0:
                    act.wait_ge(xin_landed, 16 * value)
                if k >= 3:
                    act.wait_ge(xacc_made, (value - 1) * (KD - 1) + k - 2)
                act.activation(xacc[:] if k == 0 else xsq[k % 2][:], xin[:, k, :],
                               ACT.Square).then_inc(xsq_made, 1)

            def x_norm(value):
                act.wait_ge(xssq_done, value)
                act.activation(xrs[:], B4[:, 0:T], ACT.Ln, bias=eps_t[:], scale=1.0 / D).then_inc(b4_read, 1)

            def x_norm_exp(value, b4_value):
                act.wait_ge(b4_read, b4_value)
                act.activation(xrs[:], xrs[:], ACT.Exp, scale=-0.5).then_inc(xrs_made, 1)

            def h_hi(value, k):
                act.wait_ge(h32_made, (value - 1) * KD + k + 1)
                act.activation(hhi[k][:], h32[k % 2][:], ACT.Copy).then_inc(hhi_made, 1)

            def sigmoid(t, kind, i, out, done):
                act.wait_ge(acc_done, acc_ready(t, kind, i))
                act.activation(out[:], z_bank(kind, i)[:, 0:T], ACT.Sigmoid).then_inc(done, 1)

            def decays(t, last, h):
                act.wait_ge(z_sem("f", h), z_done(t, "f", h))
                act.activation(logf[:], sf[h % 2][:], ACT.Ln, bias=lb0[:, h:h + 1],
                               scale=oml[:, h:h + 1]).then_inc(logf_made, 1)
                act.wait_ge(b_made, nth(t, H, h))
                act.activation(e3[h % 2][:], bc[:], ACT.Exp).then_inc(exp_made, 1)
                act.wait_ge(d_made, nth(t, 2 * H, 2 * h))
                act.activation(e1[:], dd[:], ACT.Exp).then_inc(exp_made, 1)
                act.activation(e2[:], dd[:], ACT.Exp, scale=-1.0).then_inc(exp_made, 1)
                act.wait_ge(d_made, nth(t, 2 * H, 2 * h + 1))
                act.activation(e4[:], dl[:], ACT.Exp).then_inc(exp_made, 1)

            def head_norm(t, h):
                act.wait_ge(ssq_done, nth(t, H, h))
                act.activation(rst[:], B4[:, 0:T], ACT.Ln, bias=eps_t[:], scale=1.0 / P).then_inc(b4_read, 1)
                act.wait_ge(b4_read, b4_done(t, "ssq", h))
                act.activation(rst[:], rst[:], ACT.Exp, scale=-0.5).then_inc(rst_made, 1)

            def tile(t, last):
                for s in range(NU):
                    if s + AHEAD < NU or not last:
                        act.wait_ge(acc_done, t * NA + (LAST_ACC[s - 1] + 1 if s else 0))
                        split(t, s + AHEAD)
                    for h in range(H):
                        if s == 4 * h + 1:
                            sigmoid(t, "f", h, sf[h % 2], z_sem("f", h))
                        if s == 4 * h + 2:
                            sigmoid(t, "q", h, qf[h % 2], sq_made)
                        if s == 4 * h + 3:
                            act.wait_ge(acc_done, acc_ready(t, "i", h))
                            act.activation(vt[:], z_bank("i", h)[:, 0:T], ACT.Copy).then_inc(z_sem("i", h), 1)
                        if s == 4 * h + 4:
                            sigmoid(t, "g", h, ga[h % 3], sg_made)
                            decays(t, last, h)
                        if s == 4 * h + 12:
                            head_norm(t, h)
                        if s == 4 * h + 6:
                            act.wait_ge(tv_done, nth(t, H, h))
                            act.activation(vtm[:, 0:3, :], B5[:, 0:3 * P].rearrange("p (g v) -> p g v", v=P), ACT.Copy)
                            act.activation(vtm[0:SAMPLE, 3, :], B5[0:SAMPLE, 3 * P:4 * P],
                                           ACT.Copy).then_inc(b5_read, 1)
                        if s == 4 * h + 9:
                            act.wait_ge(o_done, nth(t, H, h))
                            act.activation(osq[:], B5[:, 0:T], ACT.Square).then_inc(osq_made, 1)
                            act.activation(o_sb[:], B5[:, 0:T], ACT.Copy).then_inc(b5_read, 1)
                        if s == 4 * h + 13:
                            act.wait_ge(og_made, nth(t, H, h))
                            act.activation(yhi[h][:], og[h % 2][:], ACT.Copy).then_inc(yhi_made, 1)
                    for g in range(G):
                        if s == 17 + 2 * g:
                            act.wait_ge(acc_done, acc_ready(t, "u", g))
                            act.wait_ge(hist_kept, t * G)
                            z = z_bank("u", g)
                            if last:
                                act.activation(ext[:, g, BUF:BUF + PT], z[:, 0:PT], ACT.Copy)
                                act.activation(exts[:, g, :, BUF:BUF + NT],
                                               z[:, PT:T].rearrange("p (b n) -> p b n", n=NT),
                                               ACT.Copy).then_inc(z_sem("u", g), 1)
                            else:
                                act.activation(ext[:, g, BUF:EXT], z[:, 0:T], ACT.Copy).then_inc(z_sem("u", g), 1)
                        if s == 18 + 2 * g:
                            if g == 3:
                                act.wait_ge(ylo_made, nth(t, 8, Y_ORDER.index(4)))
                            sigmoid(t, "b", g, bg[g % 3], sb_made)
                    if s in MIX_SLOT:
                        g = MIX_SLOT[s]
                        act.wait_ge(ybm_made, nth(t, G, g))
                        act.activation(yhi[4 + g][:], bg[g % 3][:], ACT.Copy).then_inc(yhi_made, 1)
                    kind, j = UNITS[s - 1] if s else (None, 0)
                    if kind == "ma":
                        sigmoid(t, "ma", j, gA[j % 3], z_sem("ma", j))
                    if kind == "mb":
                        sigmoid(t, "mb", j, gB[j % 3], z_sem("mb", j))
                    if s in XSQ_SLOT and not last:
                        x_square(t + 2, XSQ_SLOT[s])
                    if s == XNORM and not last:
                        x_norm(t + 2)
                        x_norm_exp(t + 2, b4_done(t, "xssq", 0))
                    if kind == "y":
                        act.wait_ge(merged, nth(t, KD, j))
                        act.activation(mhi[j][:], mA[j % 2][:], ACT.Copy).then_inc(mhi_made, 1)
                    if s in H_SLOT and not last:
                        h_hi(t + 2, H_SLOT[s])
                    if kind == "out":
                        y_square(t, j)
                y_square(t, KD - 1)
                act.wait_ge(yssq_done, t + 1)
                act.activation(yrs[:], B5[:, 0:T], ACT.Ln, bias=eps_t[:], scale=1.0 / D).then_inc(b5_read, 1)
                act.wait_ge(b5_read, b5_done(t, "yssq", 0))
                act.activation(yrs[:], yrs[:], ACT.Exp, scale=-0.5).then_inc(yrs_made, 1)

            def y_square(t, j):
                act.wait_ge(z_sem("out", j), z_done(t, "out", j))
                if j >= 3:
                    act.wait_ge(yacc_made, nth(t, KD - 1, j - 3))
                act.activation(yacc[:] if j == 0 else ysq[j % 2][:], xres[:, j, :], ACT.Square).then_inc(ysq_made, 1)

            act.wait_ge(zeroed, ZEROED)
            for k in range(KD):
                x_square(1, k)
            for n in range(RAW):
                split(0, n)
            act.wait_ge(lb_made, 3)
            act.activation(lb[:, 3:5], lb[:, 3:5], ACT.Exp).then_inc(lbe_made, 1)
            x_norm(1)
            x_norm_exp(1, 1)
            for n in range(RAW, AHEAD):
                split(0, n)
            for k in range(KD):
                h_hi(1, k)
            act.wait_ge(lb_made, LB_STEPS)
            tile(0, False)
            with act.Fori(1, TILES - 1) as t:
                tile(t, False)
            tile(TILES - 1, True)

        @block.vector
        def _(dve):
            def split(t, n):
                dve.wait_ge(whi_made, nth(t, NU, n))
                dve.tensor_tensor(wlo[n % RING][:], wraw[n % RAW][:], whi[n % RING][:].bitcast(F32),
                                  ALU.subtract).then_inc(wlo_made, 1)

            def h_block(value, k):
                if k == 0:
                    dve.wait_ge(xrs_made, value)
                if k >= 2:
                    dve.wait_ge(hhi_made, (value - 1) * KD + k - 1)
                dve.scalar_tensor_tensor(out=h32[k % 2][:], in0=xin[:, k, :], scalar=cst[:, C_NG + k:C_NG + k + 1],
                                         in1=xrs[:], op0=ALU.mult, op1=ALU.mult).then_inc(h32_made, 1)
                dve.wait_ge(hhi_made, (value - 1) * KD + k + 1)
                dve.tensor_tensor(hlo[k][:], h32[k % 2][:], hhi[k][:].bitcast(F32), ALU.subtract).then_inc(hlo_made, 1)

            def gated(t, kind, i, out, made, scalar):
                dve.wait_ge(made, nth(t, 4, i))
                dve.scalar_tensor_tensor(out=out[:], in0=z_bank(kind, i)[:, 0:T], scalar=scalar, in1=out[:],
                                         op0=ALU.mult, op1=ALU.mult).then_inc(z_sem(kind, i), 1)

            def sums(t, last, h):
                dve.wait_ge(logf_made, nth(t, H, h))
                parts = [(0, PT, CHUNK, smask[:, 0:PT]), (PT, T, NT, smask_s[:])] if last else [(0, T, CHUNK, smask[:])]
                for lo, hi, n, mask in parts:
                    ins = dve.tensor_tensor_scan(bc[:, lo:hi], mask, logf[:, lo:hi], 0.0, ALU.mult, ALU.add)
                ins.then_inc(b_made, 1)
                dve.wait_ge(b_made, nth(t, H, h))
                for out, at, sign in ((dd, 0, 1), (dl, 1, -1)):
                    for lo, hi, n, _ in parts:
                        v = bc[:, lo:hi].rearrange("p (c n) -> p c n", n=n)
                        m = n // 2 if at == 0 else n - 1
                        r = v[:, :, m:m + 1].broadcast_to([P, (hi - lo) // n, n])
                        o = out[:, lo:hi].rearrange("p (c n) -> p c n", n=n)
                        a, b = (v, r) if sign == 1 else (r, v)
                        ins = dve.tensor_tensor(o, a, b, ALU.subtract)
                    ins.then_inc(d_made, 1)
                dve.wait_ge(z_sem("q", h), z_done(t, "q", h))
                dve.wait_ge(exp_made, nth(t, 4 * H, 4 * h))
                dve.tensor_tensor(q2[h % 2][:], qf[h % 2][:], e3[h % 2][:], ALU.mult).then_inc(q_made, 1)
                dve.wait_ge(exp_made, nth(t, 4 * H, 4 * h + 1))
                dve.tensor_tensor(e1[:], qf[h % 2][:], e1[:], ALU.mult).then_inc(q_made, 1)

            def update(t, last, h, c):
                g, j = c // 4, c % 4
                if j == 0:
                    dve.wait_ge(p_done, p_value(t, last, h, g))
                if c:
                    dve.wait_ge(s_made, s_value(t, last, h, c - 1))
                s_in = s_all[:, c, :] if c else carry[:, h, :]
                s_out = carry[:, h, :] if c == (11 if last else 12) else s_all[:, c + 1, :]
                e = c * CHUNK + CHUNK - 1
                dve.scalar_tensor_tensor(out=s_out, in0=s_in, scalar=e3[h % 2][:, e:e + 1],
                                         in1=(B6, B7)[g % 2][:, j * P:(j + 1) * P], op0=ALU.mult,
                                         op1=ALU.add).then_inc(s_made, 1)

            def p_value(t, last, h, g):
                return t * 4 * H + h * (5 if last else 4) + g + 1

            def sample_update(t, h, b):
                if b % 4 == 0:
                    dve.wait_ge(p_done, p_value(t, True, h, 3 + b // 4))
                if b == 0:
                    dve.wait_ge(s0_landed[h % 2], 16 * (h // 2 + 1))
                    if h:
                        dve.wait_ge(snew_stored, 16 * h)
                e = PT + b * NT + NT - 1
                dve.scalar_tensor_tensor(out=snew[:, b, :], in0=s0[h % 2][:, b, :], scalar=e3[h % 2][:, e:e + 1],
                                         in1=(B7, B6)[b // 4][:, (b % 4) * P:(b % 4 + 1) * P], op0=ALU.mult,
                                         op1=ALU.add).then_inc(s_made, 1)

            def means(t, last, g):
                w = WINDOWS[g]
                src, srcs = (pb, pbs) if g % 2 else (pa, pas)
                n = PT if last else T
                dve.wait_ge(win_made, win_value(t, last, g, g, last))
                if g == 0:
                    dve.wait_ge(rc_used, RC_FIRST + t)
                if g >= 2:
                    dve.wait_ge(mix_done, nth(t, G, g - 2))
                dve.tensor_tensor(ptmp[:], src[:, BUF:2 * BUF], rc[:, g, :], ALU.mult).then_inc(ptmp_made, 1)
                dve.scalar_tensor_tensor(out=pooled[g % 2][:, BUF:n], in0=src[:, 2 * BUF:BUF + n], scalar=1.0 / w,
                                         in1=ext[:, g, 2 * BUF:BUF + n], op0=ALU.mult, op1=ALU.subtract)
                if last:
                    dve.scalar_tensor_tensor(
                        out=pooled[g % 2][:, PT:T].rearrange("p (b n) -> p b n", n=NT), in0=srcs[:, :, BUF:BUF + NT],
                        scalar=1.0 / w, in1=exts[:, g, :, BUF:BUF + NT], op0=ALU.mult, op1=ALU.subtract)
                dve.wait_ge(ptmp_made, nth(t, G, g))
                dve.tensor_tensor(pooled[g % 2][:, 0:BUF], ptmp[:], ext[:, g, BUF:2 * BUF],
                                  ALU.subtract).then_inc(pooled_made, 1)
                if not last:
                    dve.wait_ge(pooled_made, nth(t, G, g))
                    dve.tensor_copy(ext[:, g, 0:BUF], ext[:, g, T:T + BUF]).then_inc(hist_kept, 1)

            def merge(t, j):
                for acc, gate, out, n in (("ya", gA, mA, 0), ("yb", gB, mB, 1)):
                    dve.wait_ge(acc_done, acc_ready(t, acc, j))
                    dve.wait_ge(z_sem("m" + acc[1], j), z_done(t, "m" + acc[1], j))
                    dve.tensor_tensor(out[j % 2][:], z_bank(acc, j)[:, 0:T], gate[j % 3][:],
                                      ALU.mult).then_inc(z_sem(acc, j), 1)
                dve.wait_ge(mhi_made, nth(t, KD, j))
                dve.tensor_tensor(mlo[j][:], mA[j % 2][:], mhi[j][:].bitcast(F32), ALU.subtract).then_inc(mlo_made, 1)

            def residual(t, j):
                if j == 0:
                    dve.wait_ge(xres_landed, 16 * t + 16)
                dve.wait_ge(acc_done, acc_ready(t, "out", j))
                dve.tensor_tensor(xres[:, j, :], z_bank("out", j)[:, 0:T], xres[:, j, :],
                                  ALU.add).then_inc(z_sem("out", j), 1)

            def tile(t, last):
                for s in range(NU):
                    if s + AHEAD < NU or not last:
                        split(t, s + AHEAD)
                    for h in range(H):
                        if s == 4 * h + 1:
                            dve.wait_ge(z_sem("f", h), z_done(t, "f", h))
                            dve.tensor_scalar(kin[h % 2][:], sf[h % 2][:], noml[:, h:h + 1], oml[:, h:h + 1],
                                              ALU.mult, ALU.add).then_inc(kin_made, 1)
                        if s == 4 * h + 2:
                            gated(t, "q", h, qf[h % 2], sq_made, QSCALE)
                        if s == 4 * h + 4:
                            gated(t, "g", h, ga[h % 3], sg_made, cst[:, C_GN:C_GN + 1])
                            sums(t, last, h)
                        if s == 4 * h + 6:
                            dve.wait_ge(b5_read, b5_done(t, "tv", h))
                            for j in range(4):
                                ng = 4 if j == 0 and not last else 3
                                r = slice(CHUNK * j, CHUNK * (j + 1))
                                dve.tensor_copy(vbd[r, 0:ng, j, :], vtm[r, 0:ng, :]).then_inc(vbd_made, 1)
                            dve.wait_ge(tk_done, nth(t, H, h))
                            dve.tensor_copy(ktm[:, 0:3, :], B4[:, 0:3 * P].rearrange("p (g v) -> p g v", v=P))
                            dve.tensor_copy(ktm[0:SAMPLE, 3, :], B4[0:SAMPLE, 3 * P:4 * P]).then_inc(b4_read, 1)
                            if last:
                                for half, out in enumerate((vbd[0:SAMPLE, 3], vms[0:SAMPLE])):
                                    dve.tensor_tensor(
                                        out, vtm[0:SAMPLE, 3:4, :].broadcast_to([SAMPLE, 4, P]),
                                        bmask[0:SAMPLE, 4 * half:4 * half + 4].unsqueeze(2).broadcast_to([SAMPLE, 4, P]),
                                        ALU.mult).then_inc(vms_made, 1)
                        if s == 4 * h + 7:
                            dve.wait_ge(sc_done, nth(t, H, h))
                            dve.wait_ge(o_done, t * H + h)
                            if h == 0:
                                dve.wait_ge(s_made, t * H * NC)
                            dve.tensor_copy(s_all[:, 0, :], carry[:, h, :]).then_inc(s0_copied, 1)
                            dve.copy_predicated(at_sb[:, 0:PT], cmask[:].bitcast(U32).rearrange("p a b c -> p (a b c)"),
                                                B4[:, 0:PT])
                            out3, mask3 = (ats[0:SAMPLE, :], cmask_s[0:SAMPLE]) if last else (
                                at_sb[0:SAMPLE, PT:T], cmask[0:SAMPLE, 0, 0:1, :])
                            dve.copy_predicated(out3, mask3.bitcast(U32).rearrange("p a b -> p (a b)"),
                                                B4[0:SAMPLE, PT:T]).then_inc(b4_read, 1)
                            for c in range(8):
                                update(t, last, h, c)
                        if s == 4 * h + 8:
                            for c in range(8, 12 if last else NC):
                                update(t, last, h, c)
                            if last:
                                for b in range(4):
                                    sample_update(t, h, b)
                        if s == 4 * h + 9 and last:
                            for b in range(4, NB):
                                sample_update(t, h, b)
                        if s == 4 * h + 12:
                            dve.wait_ge(b5_read, b5_done(t, "o", h))
                            dve.wait_ge(rst_made, nth(t, H, h))
                            dve.tensor_tensor(og[h % 2][:], o_sb[:], rst[:], ALU.mult).then_inc(t1_made, 1)
                            dve.wait_ge(t1_made, nth(t, H, h))
                            dve.tensor_tensor(og[h % 2][:], og[h % 2][:], ga[h % 3][:], ALU.mult).then_inc(og_made, 1)
                        if s == 4 * h + 13:
                            dve.wait_ge(yhi_made, nth(t, 8, Y_ORDER.index(h)))
                            dve.tensor_tensor(ylo[h][:], og[h % 2][:], yhi[h][:].bitcast(F32),
                                              ALU.subtract).then_inc(ylo_made, 1)
                    for g in range(G):
                        if s == 18 + 2 * g:
                            gated(t, "b", g, bg[g % 3], sb_made, cst[:, C_PS + g:C_PS + g + 1])
                        if s == 18 + 2 * g:
                            means(t, last, g)
                    if s in MIX_SLOT:
                        g = MIX_SLOT[s]
                        dve.wait_ge(mix_done, nth(t, G, g))
                        dve.wait_ge(z_sem("b", g), z_done(t, "b", g))
                        dve.tensor_tensor(bg[g % 3][:], (B6, B7)[g % 2][:, 0:T], bg[g % 3][:],
                                          ALU.mult).then_inc(ybm_made, 1)
                        dve.wait_ge(yhi_made, nth(t, 8, Y_ORDER.index(4 + g)))
                        dve.tensor_tensor(ylo[4 + g][:], bg[g % 3][:], yhi[4 + g][:].bitcast(F32),
                                          ALU.subtract).then_inc(ylo_made, 1)
                    kind, j = UNITS[s - 1] if s else (None, 0)
                    if kind == "y":
                        merge(t, j)
                    if kind == "out":
                        residual(t, j)
                    if s in H_SLOT and not last:
                        h_block(t + 2, H_SLOT[s])
                    if s == 27 and not last:
                        for g in range(G):
                            ins = dve.memset(rc[:, g, :], 1.0 / WINDOWS[g])
                        ins.then_inc(rc_used, 1)
                residual(t, KD - 1)
                dve.wait_ge(yrs_made, t + 1)
                for j in range(KD):
                    dve.scalar_tensor_tensor(out=xres[:, j, :], in0=xres[:, j, :],
                                             scalar=cst[:, C_FG + j:C_FG + j + 1], in1=yrs[:], op0=ALU.mult,
                                             op1=ALU.mult).then_inc(y_made, 1)

            zero = [ext[:, :, 0:BUF], carry[:], vbd[:], at_sb[:], ats[:]]
            for z in zero:
                dve.memset(z, 0.0).then_inc(zeroed, 1)
            dve.memset(eps_t[:], EPS).then_inc(zeroed, 1)

            for n in range(RAW):
                split(0, n)
            dve.wait_ge(cst_landed, 32)
            l0, l1 = cst[:, C_LB:C_LB + H], cst[:, C_LB + H:C_LB + 2 * H]
            dve.tensor_tensor(lb[:, 5], l0, l1, ALU.max).then_inc(lb_made, 1)
            dve.wait_ge(lb_made, 1)
            dve.tensor_tensor(lb[:, 3], l0, lb[:, 5], ALU.subtract).then_inc(lb_made, 1)
            dve.tensor_tensor(lb[:, 4], l1, lb[:, 5], ALU.subtract).then_inc(lb_made, 1)
            dve.wait_ge(lbe_made, 1)
            dve.tensor_tensor(lb[:, 6], lb[:, 3], lb[:, 4], ALU.add).then_inc(lb_made, 1)
            dve.wait_ge(lb_made, 4)
            dve.reciprocal(lb[:, 7], lb[:, 6]).then_inc(lb_made, 1)
            dve.wait_ge(lb_made, 5)
            dve.tensor_tensor(lb[:, 0], lb[:, 3], lb[:, 7], ALU.mult).then_inc(lb_made, 1)
            dve.wait_ge(lb_made, 6)
            dve.tensor_scalar(lb[:, 1], lb[:, 0], -1.0, 1.0, ALU.mult, ALU.add).then_inc(lb_made, 1)
            dve.wait_ge(lb_made, 7)
            dve.tensor_scalar(lb[:, 2], lb[:, 1], -1.0, None, ALU.mult).then_inc(lb_made, 1)
            dve.wait_ge(masks, MASKS)
            for g in range(G):
                dve.tensor_scalar(rc[:, g, :], rc[:, g, :], float(WINDOWS[g]), None, ALU.min).then_inc(rc_used, 1)
            dve.wait_ge(rc_used, G)
            dve.reciprocal(rc[:], rc[:]).then_inc(rc_used, 1)
            for n in range(RAW, AHEAD):
                split(0, n)
            for k in range(KD):
                h_block(1, k)
            dve.wait_ge(lb_made, LB_STEPS)
            tile(0, False)
            with dve.Fori(1, TILES - 1) as t:
                tile(t, False)
            tile(TILES - 1, True)

        @block.gpsimd
        def _(pool):
            count = [0]

            def step(ins):
                ins.then_inc(masks, 1)
                count[0] += 1
                pool.wait_ge(masks, count[0])

            def x_sum(value, k):
                pool.wait_ge(xsq_made, (value - 1) * KD + k + 1)
                if k > 1:
                    pool.wait_ge(xacc_made, (value - 1) * (KD - 1) + k - 1)
                pool.tensor_tensor(xacc[:], xacc[:], xsq[k % 2][:], ALU.add).then_inc(xacc_made, 1)

            def y_sum(t, j):
                pool.wait_ge(ysq_made, nth(t, KD, j))
                if j > 1:
                    pool.wait_ge(yacc_made, nth(t, KD - 1, j - 2))
                pool.tensor_tensor(yacc[:], yacc[:], ysq[j % 2][:], ALU.add).then_inc(yacc_made, 1)

            def wins(level):
                return lambda lo, hi: (pa, pb)[level % 2][:, lo:hi]

            def windows(t, last, g):
                pool.wait_ge(z_sem("u", g), z_done(t, "u", g))
                if g == 0 and last:
                    pool.wait_ge(buf_landed, 16)
                if g >= 1:
                    pool.wait_ge(pooled_made, pooled_value(t, last, g - 1))
                for level in range(g + 1):
                    w = 1 << level
                    n = PT if last else T
                    if level:
                        pool.wait_ge(win_made, win_value(t, last, g, level - 1, last))
                    first = 2 * w - 1
                    if level == 0:
                        a = ext[:, g, first:BUF + n]
                        b = ext[:, g, first - w:BUF + n - w]
                    else:
                        src = wins(level - 1)
                        a, b = src(first, BUF + n), src(first - w, BUF + n - w)
                    pool.tensor_tensor(wins(level)(first, BUF + n), a, b, ALU.add).then_inc(win_made, 1)
                    if last:
                        e = BUF + NT
                        if level == 0:
                            a, b = exts[:, g, :, first:e], exts[:, g, :, first - w:e - w]
                        else:
                            ss = (pas, pbs)[(level - 1) % 2]
                            a, b = ss[:, :, first:e], ss[:, :, first - w:e - w]
                        pool.tensor_tensor((pas, pbs)[level % 2][:, :, first:e], a, b, ALU.add).then_inc(win_made, 1)

            def tile(t, last):
                for s in range(NU):
                    for h in range(H):
                        if s == 4 * h + 4:
                            pool.wait_ge(kin_made, nth(t, H, h))
                            pool.wait_ge(exp_made, nth(t, 4 * H, 4 * h + 2))
                            pool.tensor_tensor(e2[:], kin[h % 2][:], e2[:], ALU.mult).then_inc(k_made, 1)
                            pool.wait_ge(exp_made, nth(t, 4 * H, 4 * h + 3))
                            pool.tensor_tensor(e4[:], kin[h % 2][:], e4[:], ALU.mult).then_inc(k_made, 1)
                    for g in range(G):
                        if s == 17 + 2 * g:
                            windows(t, last, g)
                    kind, j = UNITS[s - 1] if s else (None, 0)
                    if kind == "y":
                        pool.wait_ge(z_sem("yb", j), z_done(t, "yb", j))
                        pool.wait_ge(z_sem("ya", j), z_done(t, "ya", j))
                        pool.tensor_tensor(mA[j % 2][:], mA[j % 2][:], mB[j % 2][:], ALU.add).then_inc(merged, 1)
                    if s in XSQ_SLOT and not last and XSQ_SLOT[s]:
                        x_sum(t + 2, XSQ_SLOT[s])
                    if kind == "out" and j:
                        y_sum(t, j)
                y_sum(t, KD - 1)
                pool.wait_ge(y_made, nth(t, KD, KD - 1))
                pool.dma_start(yT[t], xres[:]).then_inc(y_stored, 16)

            for value, m in ((1.0, ones[:]), (0.0, ident[:]), (1.0, cmask[:]), (1.0, cmask_s[:]), (1.0, bmask[:]),
                             (1.0, smask[:]), (1.0, smask_s[:])):
                step(pool.memset(m, value))
            step(pool.affine_select(out=ident[:], in_=ident[:], compare_op=ALU.not_equal, fill=1.0, base=0,
                                    pattern=[[-1, P]], channel_multiplier=1))
            step(pool.memset(smask[:].rearrange("p (c n) -> p c n", n=CHUNK)[:, :, 0:1], 0.0))
            step(pool.memset(smask_s[:].rearrange("p (c n) -> p c n", n=NT)[:, :, 0:1], 0.0))
            for g in range(3):
                m = cmask[:, g]
                step(pool.affine_select(out=m, in_=m, compare_op=ALU.is_ge, fill=0.0, base=0,
                                        pattern=[[CHUNK, 4], [1, CHUNK]], channel_multiplier=-1))
                step(pool.affine_select(out=m, in_=m, compare_op=ALU.is_ge, fill=0.0, base=0,
                                        pattern=[[-CHUNK, 4], [0, CHUNK]], channel_multiplier=1))
            m = cmask_s[:]
            step(pool.affine_select(out=m, in_=m, compare_op=ALU.is_ge, fill=0.0, base=0,
                                    pattern=[[NT, NB], [1, NT]], channel_multiplier=-1))
            step(pool.affine_select(out=m, in_=m, compare_op=ALU.is_ge, fill=0.0, base=0,
                                    pattern=[[-NT, NB], [0, NT]], channel_multiplier=1))
            step(pool.affine_select(out=bmask[:], in_=bmask[:], compare_op=ALU.is_ge, fill=0.0, base=0,
                                    pattern=[[-NT, NB]], channel_multiplier=1))
            step(pool.affine_select(out=bmask[:], in_=bmask[:], compare_op=ALU.is_ge, fill=0.0, base=NT - 1,
                                    pattern=[[NT, NB]], channel_multiplier=-1))
            step(pool.iota(rc[:], pattern=[[0, G], [1, BUF]], base=1, channel_multiplier=0,
                           allow_small_or_imprecise_dtypes=True))
            assert count[0] == MASKS
            for k in range(1, KD):
                x_sum(1, k)
            tile(0, False)
            with pool.Fori(1, TILES - 1) as t:
                tile(t, False)
            tile(TILES - 1, True)


def column_block(w, c):
    k = w.shape[0] // P
    return w[:, c:c + P].reshape(k, P, P).transpose(1, 0, 2).reshape(P, k * P)


def kernel(x_prompt, x_sample, state_hgrn, state_pool, norm_g, w_in, lb_logits, hgrn_norm_g, w_proj_a, w_pool,
           pool_scale, w_proj_b, w_out, final_norm_g):
    import concourse.bacc as bacc
    from concourse.bass_utils import run_bass_kernel_spmd

    a = [np.asarray(v) for v in (x_prompt, x_sample, state_hgrn, state_pool, norm_g, w_in, lb_logits, hgrn_norm_g,
                                 w_proj_a, w_pool, pool_scale, w_proj_b, w_out, final_norm_g)]
    (xp, xs, sh, spl, ng, win, lbl, hn, wa, wp, psc, wb, wo, fg) = a
    win, wa, wb, wo = win[0], wa[0], wb[0], wo[0]
    x = np.concatenate([xp.reshape(SEQ, D), xs.reshape(SAMPLE, D)]).reshape(TILES, T, KD, P).transpose(0, 3, 2, 1)
    width = D // 2
    first = {"q": 0, "f": width, "i": 2 * width, "g": 3 * width, "u": 4 * width, "b": 5 * width,
             "ma": 6 * width, "mb": 6 * width + D}
    blocks = []
    for kind, i in UNITS:
        if kind == "y":
            blocks.append(np.concatenate([column_block(wa, i * P), column_block(wb, i * P)], axis=1))
        elif kind == "out":
            blocks.append(column_block(wo, i * P))
        else:
            blocks.append(column_block(win, first[kind] + i * P))
    consts = np.concatenate([ng.reshape(KD, P).T, hn.reshape(1, P).T, psc.reshape(G, P).T, fg.reshape(KD, P).T,
                             lbl.reshape(2, H, P).transpose(2, 0, 1).reshape(P, 2 * H)], axis=1)
    arrays = {
        "xT": x, "w_all": np.stack(blocks), "consts": consts, "w_pool": wp[0].transpose(1, 0, 2),
        "s_in": sh[0].transpose(1, 2, 0, 3), "buf_in": spl[0].reshape(NB, BUF, G, P).transpose(3, 2, 0, 1),
    }
    arrays = {n: np.ascontiguousarray(v) for n, v in arrays.items()}
    outs = {"yT": x.shape, "sp_out": (P, H, P), "pp_out": (P, G, BUF), "ss_out": (H, P, NB, P),
            "ps_out": (P, G, NB, BUF)}
    nc = bacc.Bacc("TRN2", target_bir_lowering=False, num_devices=1)
    args = [nc.dram_tensor(n, v.shape, mybir.dt.from_np(v.dtype), kind="ExternalInput").ap()
            for n, v in arrays.items()]
    args += [nc.dram_tensor(n, v, F32, kind="ExternalOutput").ap() for n, v in outs.items()]
    step_kernel(nc, *args)
    r = run_bass_kernel_spmd(nc, [arrays], core_ids=[0]).results[0]
    y = np.asarray(r["yT"]).transpose(0, 3, 2, 1).reshape(SEQ + SAMPLE, D)
    return (
        np.ascontiguousarray(y[:SEQ]).reshape(1, SEQ, D),
        np.ascontiguousarray(y[SEQ:]).reshape(NB, NT, D),
        np.ascontiguousarray(np.asarray(r["sp_out"]).transpose(1, 0, 2)).reshape(1, 1, H, P, P),
        np.ascontiguousarray(np.asarray(r["pp_out"]).transpose(2, 1, 0)).reshape(1, 1, BUF, G * P),
        np.ascontiguousarray(np.asarray(r["ss_out"]).transpose(2, 0, 1, 3)).reshape(1, NB, H, P, P),
        np.ascontiguousarray(np.asarray(r["ps_out"]).transpose(2, 3, 1, 0)).reshape(1, NB, BUF, G * P),
    )
```

```python
from contextlib import ExitStack

import numpy as np

import concourse.bass as bass
from concourse import mybir

F32 = mybir.dt.float32
F32R = mybir.dt.float32r
U32 = mybir.dt.uint32
ALU = mybir.AluOpType
ACT = mybir.ActivationFunctionType

P = 128
D = 1024
KD = D // P
SEQ = 2048
NB, NT = 8, 4
SAMPLE = NB * NT
T = 416
TILES = (SEQ + SAMPLE) // T
H = 4
G = 4
CHUNK = 32
NG = 3
PT = T - SAMPLE
BUF = 15
WINDOWS = (2, 4, 8, 16)
EPS = 1e-6
QSCALE = float(P) ** -0.5
RAW = 2
RING = 4
AHEAD = RING - 1

UNITS = [(kind, h) for h in range(H) for kind in "fqig"]
UNITS += [(kind, g) for g in range(G) for kind in "ub"]
UNITS += [("ma", 0), ("mb", 0)]
for _j in range(1, KD):
    UNITS += [("ma", _j), ("mb", _j), ("y", _j - 1)]
UNITS += [("y", KD - 1)]
UNITS += [("out", _j) for _j in range(KD)]
NU = len(UNITS)
SLOT = {u: s for s, u in enumerate(UNITS)}

ACCS = []
for _kind, _i in UNITS:
    ACCS += [("ya", _i), ("yb", _i)] if _kind == "y" else [(_kind, _i)]
NA = len(ACCS)
ACC = {a: n for n, a in enumerate(ACCS)}
NZ = 4
LAST_ACC = [ACC[("yb", i)] if kind == "y" else ACC[(kind, i)] for kind, i in UNITS]

MIX_SLOT = {22: 0, 23: 1, 25: 2, 26: 3}
XSQ_SLOT = {28 + 2 * k: k for k in range(KD)}
XNORM = 46
H_SLOT = {47 + k: k for k in range(KD)}

B4_USES, B5_USES = [], []
for _s in range(NU):
    for _h in range(H):
        if _s == 4 * _h + 12:
            B4_USES.append(("ssq", _h))
        if _s == 4 * _h + 6:
            B4_USES.append(("tk", _h))
            B5_USES.append(("tv", _h))
        if _s == 4 * _h + 7:
            B4_USES.append(("scores", _h))
        if _s == 4 * _h + 9:
            B5_USES.append(("o", _h))
    if _s == XNORM:
        B4_USES.append(("xssq", 0))
B5_USES.append(("yssq", 0))

C_NG, C_GN, C_PS, C_FG, C_LB = 0, 8, 9, 13, 21
C_N = 29

Y_ORDER = [k for _, k in sorted([(4 * h + 13, h) for h in range(H)]
                                + [(s + 0.5, 4 + g) for s, g in MIX_SLOT.items()])]
MASKS = 18
ZEROED = 6
LN_EXP = "natural_log_exp_and_others"
LB_STEPS = 8
RC_FIRST = G + 1
YNORM = 3


def step_kernel(nc, xT, w_all, consts, w_pool, s_in, buf_in, yT, sp_out, pp_out, ss_out, ps_out):
    with ExitStack() as ctx:
        start = (int(nc.sbuf_base) + 63) // 64 * 64
        top = [start]

        def put(name, shape, dt=F32, at=None, parts=P):
            size = 4 * int(np.prod(shape))
            if at is None:
                at = top[0]
                top[0] += (size + 31) // 32 * 32
            return nc.alloc_sbuf_tensor_at(name, [parts, *shape], dt, offset=at)

        def region(size):
            at = top[0]
            top[0] += (size + 31) // 32 * 32
            return at

        B = 4 * T
        wraw = [put(f"wraw{i}", [D]) for i in range(RAW)]
        whi = [put(f"whi{i}", [D], F32R) for i in range(RING)]
        wlo = [put(f"wlo{i}", [D], F32R) for i in range(RING)]
        hhi = [put(f"hhi{k}", [T], F32R) for k in range(KD)]
        hlo = [put(f"hlo{k}", [T], F32R) for k in range(KD)]
        yhi = [put(f"yhi{k}", [T], F32R) for k in range(KD)]
        ylo = [put(f"ylo{k}", [T], F32R) for k in range(KD)]
        r1 = region(16 * B)
        mhi = [put(f"mhi{k}", [T], F32R, r1 + k * B) for k in range(KD)]
        mlo = [put(f"mlo{k}", [T], F32R, r1 + (KD + k) * B) for k in range(KD)]
        r2 = region(KD * B)
        xin = put("xin", [KD, T], F32, r2)
        own = region(2 * B)
        hg = [r1 + i * B for i in range(16)] + [r2 + i * B for i in range(8)] + [own, own + B]
        names = ["b", "d", "dl", "e1", "e2", "e4", "e30", "e31", "q20", "q21", "ga0", "ga1", "ga2", "os",
                 "osq", "rst", "og0", "og1", "sf0", "sf1", "qf0", "qf1", "kin0", "kin1", "vt", "logf"]
        buf = {n: put("h_" + n, [T], F32, at) for n, at in zip(names, hg)}
        sf = [buf["sf0"], buf["sf1"]]
        qf = [buf["qf0"], buf["qf1"]]
        kin = [buf["kin0"], buf["kin1"]]
        ga = [buf["ga0"], buf["ga1"], buf["ga2"]]
        e3 = [buf["e30"], buf["e31"]]
        q2 = [buf["q20"], buf["q21"]]
        og = [buf["og0"], buf["og1"]]
        vt, logf, bc, dd, dl = buf["vt"], buf["logf"], buf["b"], buf["d"], buf["dl"]
        e1, e2, e4 = buf["e1"], buf["e2"], buf["e4"]
        o_sb, osq, rst = buf["os"], buf["osq"], buf["rst"]
        r3 = region(10 * B + 128)
        gA = [put(f"gA{i}", [T], F32, r3 + a * B) for i, a in enumerate((0, 2, 4))]
        gB = [put(f"gB{i}", [T], F32, r3 + a * B) for i, a in enumerate((1, 3, 5))]
        mA = [put(f"mA{i}", [T], F32, r3 + (6 + i) * B) for i in range(2)]
        mB = [put(f"mB{i}", [T], F32, r3 + (8 + i) * B) for i in range(2)]
        s_all = put("s_all", [4, P], F32, r3)
        psq = [put(f"psq{k}", [T], F32, r3 + k * B) for k in range(KD)]
        bg_own = region(B)
        bg = [put("bg0", [T], F32, bg_own), put("bg1", [T], F32, r3 + 4 * B), put("bg2", [T], F32, r3 + 5 * B)]
        pa = put("pa", [BUF + T], F32, r3 + 6 * B)
        pb = put("pb", [BUF + T], F32, r3 + 6 * B + 1728)
        pooled = [put(f"pooled{i}", [T], F32, r3 + 6 * B + 3456 + i * B) for i in range(2)]
        h32 = [put(f"h32_{i}", [T], F32, r3 + (4 + i) * B) for i in range(2)]
        ysq = [put(f"ysq{i}", [T], F32, r3 + i * B) for i in range(2)]
        yacc = put("yacc", [T], F32, r3 + 6 * B)
        yrs = put("yrs", [T], F32, r3 + 8 * B)
        xsq = [put(f"xsq{i}", [T]) for i in range(2)]
        xacc = put("xacc", [T])
        xrs = xsq[0]
        xr_at = region(KD * B)
        xres = put("xres", [KD, T], F32, xr_at)
        s0 = [put(f"s0_{i}", [NB, P], F32, xr_at + 4096 * i) for i in range(2)]
        snew = put("snew", [NB, P], F32, xr_at + 8192)
        ktm = put("ktm", [4, P])
        vtm = put("vtm", [4, P])
        vms = [put(f"vms{i}", [4, P]) for i in range(2)]
        kj2 = put("kj2", [NG, 2, CHUNK])
        kj3 = put("kj3", [NG, 3, CHUNK])
        kj4 = put("kj4", [NG, 4, CHUNK])
        q4 = [put(f"q4_{i}", [NG, 4, CHUNK]) for i in range(2)]
        dprev = put("dprev", [NG, 4])
        dfirst = put("dfirst", [NG, 4])
        dq = put("dq", [NG, 4])
        dg = put("dg", [NG])
        at_sb = put("at_sb", [T])
        ats = put("ats", [SAMPLE])
        carry = put("carry", [H, P])
        EXT = BUF + T
        ext = put("ext", [G, EXT])
        exts = put("exts", [G, NB, BUF + NT])
        pas = put("pas", [NB, BUF + NT])
        pbs = put("pbs", [NB, BUF + NT])
        wpl = put("wpl", [G, P])
        cst = put("cst", [C_N])
        smask = put("smask", [T])
        smask_s = put("smask_s", [SAMPLE])
        cmask = put("cmask", [NG, P])
        cmask_s = put("cmask_s", [NB, NT])
        bmask = put("bmask", [NB])
        ones = put("ones", [P])
        ident = put("ident", [P])
        lb = put("lb", [8, H])
        eps_t = put("eps_t", [1])
        rc = put("rc", [G, BUF])
        ptmp = put("ptmp", [BUF])
        assert top[0] <= nc.sbuf_usable_end, (top[0], nc.sbuf_usable_end)
        lb0, oml, noml = lb[:, 0], lb[:, 1], lb[:, 2]

        Z = [ctx.enter_context(nc.psum_tensor(f"Z{i}", [P, 512], F32)) for i in range(NZ)]
        B4, B5, B6, B7 = [ctx.enter_context(nc.psum_tensor(f"B{i}", [P, 512], F32)) for i in range(4, 8)]

        def sem(name):
            return ctx.enter_context(nc.semaphore(name))

        w_landed = [sem(f"w_landed{i}") for i in range(RAW)]
        x0_landed = [sem(f"x0_landed{i}") for i in range(4)]
        xin_landed, xres_landed, cst_landed = sem("xin_landed"), sem("xres_landed"), sem("cst_landed")
        s0_landed, buf_landed = [sem(f"s0_landed{i}") for i in range(2)], sem("buf_landed")
        y_stored, snew_stored, ends_stored = sem("y_stored"), sem("snew_stored"), sem("ends_stored")
        acc_done, tv_done, tk_done, sc_done = sem("acc_done"), sem("tv_done"), sem("tk_done"), sem("sc_done")
        p_done, o_done, ssq_done, mix_done = sem("p_done"), sem("o_done"), sem("ssq_done"), sem("mix_done")
        xssq_done, yssq_done = sem("xssq_done"), sem("yssq_done")
        whi_made, sq_made, sg_made, sb_made = sem("whi_made"), sem("sq_made"), sem("sg_made"), sem("sb_made")
        logf_made, exp_made, osq_made, rst_made = sem("logf_made"), sem("exp_made"), sem("osq_made"), sem("rst_made")
        xsq_made, xrs_made, hhi_made = sem("xsq_made"), sem("xrs_made"), sem("hhi_made")
        yhi_made, mhi_made, ysq_made, yrs_made = sem("yhi_made"), sem("mhi_made"), sem("ysq_made"), sem("yrs_made")
        yln_made, lbe_made = sem("yln_made"), sem("lbe_made")
        wlo_made, kin_made, b_made, d_made = sem("wlo_made"), sem("kin_made"), sem("b_made"), sem("d_made")
        q_made, s_made, s0_copied, og_made = sem("q_made"), sem("s_made"), sem("s0_copied"), sem("og_made")
        t1_made, ylo_made, rc_used, pooled_made = sem("t1_made"), sem("ylo_made"), sem("rc_used"), sem("pooled_made")
        hist_kept, ybm_made, mul_made, mlo_made = sem("hist_kept"), sem("ybm_made"), sem("mul_made"), sem("mlo_made")
        h32_made, hlo_made, y_made, vms_made = sem("h32_made"), sem("hlo_made"), sem("y_made"), sem("vms_made")
        lb_made, zeroed, ptmp_made = sem("lb_made"), sem("zeroed"), sem("ptmp_made")
        kj_made, dq_made = sem("kj_made"), sem("dq_made")
        k_made, win_made, merged = sem("k_made"), sem("win_made"), sem("merged")
        xacc_made, yacc_made, masks = sem("xacc_made"), sem("yacc_made"), sem("masks")
        z_read = [sem(f"z_read{i}") for i in range(NZ)]
        b4_read, b5_read = sem("b4_read"), sem("b5_read")

        def first(t):
            return isinstance(t, int) and t == 0

        def nth(t, per, i):
            return t * per + (i + 1)

        def acc_ready(t, kind, i):
            return nth(t, NA, ACC[(kind, i)])

        def z_bank(kind, i):
            return Z[ACC[(kind, i)] % NZ]

        def z_sem(kind, i):
            return z_read[ACC[(kind, i)] % NZ]

        def z_done(t, kind, i):
            return nth(t, NA // NZ, ACC[(kind, i)] // NZ)

        def b4_done(t, use, h):
            return nth(t, len(B4_USES), B4_USES.index((use, h))) + 1

        def b5_done(t, use, h):
            return nth(t, len(B5_USES), B5_USES.index((use, h)))

        def landed(t, n):
            return 16 * (t * (NU // RAW) + n // RAW + 1)

        def s_value(t, last, h, i):
            return t * 4 * H + h * (NG + NB if last else 4) + i + 1

        def p_value(t, last, h, i):
            return t * H + h * (3 if last else 1) + i + 1

        def win_value(t, last, g, level, sample=False):
            before = sum(range(1, g + 1)) * (2 if last else 1)
            return t * 10 + before + (2 * level + sample if last else level) + 1

        def pooled_value(t, last, g):
            return t * G + g + 1

        block = ctx.enter_context(nc.Block())

        @block.sync
        def _(sp):
            for i in range(4):
                sp.dma_start(xin[:, 2 * i:2 * i + 2, :], xT[0, :, 2 * i:2 * i + 2, :]).then_inc(x0_landed[i], 16)
                if i == 0:
                    sp.dma_start(cst[:], consts).then_inc(cst_landed, 16)
            for n in range(RAW):
                sp.dma_start(wraw[n][:], w_all[n]).then_inc(w_landed[n], 16)
            sp.dma_start(wpl[:], w_pool).then_inc(cst_landed, 16)
            sp.dma_start(exts[:, :, :, 0:BUF], buf_in).then_inc(buf_landed, 16)

            def tile(t, last):
                for s in range(NU):
                    if s == 9 and last:
                        sp.wait_ge(y_stored, 16 * (TILES - 1))
                        for h in range(2):
                            sp.dma_start(s0[h][:], s_in[h]).then_inc(s0_landed[h], 16)
                    n = s + RAW
                    if n < NU or not last:
                        sp.wait_ge(wlo_made, nth(t, NU, s))
                        sp.dma_start(wraw[n % RAW][:], w_all[n % NU]).then_inc(w_landed[n % RAW], 16)
                    if s == 29 and not last:
                        sp.wait_ge(ylo_made, nth(t, 8, 7))
                        sp.dma_start(xin[:], xT[t + 1]).then_inc(xin_landed, 16)
                    if s == 8 and not first(t):
                        y_store(t - 1)
                    if last and s in (14, 18, 22, 26):
                        h = (s - 14) // 4
                        sp.wait_ge(s_made, s_value(t, last, h, NG + NB - 1))
                        sp.dma_start(ss_out[h], snew[:]).then_inc(snew_stored, 16)
                        if h < 2:
                            sp.wait_ge(o_done, nth(t, H, h))
                            sp.dma_start(s0[h][:], s_in[h + 2]).then_inc(s0_landed[h], 16)
                    if s == 32:
                        if last:
                            sp.wait_ge(snew_stored, 16 * H)
                        else:
                            sp.wait_ge(y_stored, t * 16)
                        sp.dma_start(xres[:], xT[t]).then_inc(xres_landed, 16)
                if last:
                    sp.dma_start(sp_out, carry[:]).then_inc(ends_stored, 16)
                    sp.wait_ge(ybm_made, nth(t, G, G - 1))
                    sp.dma_start(pp_out, ext[:, :, PT:PT + BUF]).then_inc(ends_stored, 16)
                    sp.dma_start(ps_out, exts[:, :, :, NT:NT + BUF]).then_inc(ends_stored, 16)
                    for i in range(4):
                        sp.wait_ge(y_made, nth(t, KD, 2 * i + 1))
                        sp.dma_start(yT[t, :, 2 * i:2 * i + 2, :], xres[:, 2 * i:2 * i + 2, :]).then_inc(y_stored, 16)
                    sp.wait_ge(ends_stored, 48)
                    sp.wait_ge(snew_stored, 16 * H)
                    sp.wait_ge(y_stored, 16 * (TILES + 3))

            def y_store(t):
                sp.wait_ge(y_made, nth(t, KD, KD - 1))
                sp.dma_start(yT[t], xres[:]).then_inc(y_stored, 16)

            tile(0, False)
            with sp.Fori(1, TILES - 1) as t:
                tile(t, False)
            tile(TILES - 1, True)

        @block.tensor
        def _(pe):
            def three(out, parts, k_rhs, first, final):
                (wh, wl), (xh, xl) = parts, k_rhs
                pe.matmul(out, wh, xh, start=first, stop=False)
                pe.matmul(out, wh, xl, start=False, stop=False)
                return pe.matmul(out, wl, xh, start=False, stop=final)

            def small(t, last, s):
                for h in range(H):
                    base = 4 * h
                    if s == base + 12:
                        pe.wait_ge(osq_made, nth(t, H, h))
                        pe.wait_ge(b4_read, b4_done(t, "ssq", h) - 1)
                        pe.matmul(B4[:, 0:T], ones[:], osq[:], start=True, stop=True).then_inc(ssq_done, 1)
                    if s == base + 6:
                        pe.wait_ge(z_sem("i", h), z_done(t, "i", h))
                        pe.wait_ge(b5_read, b5_done(t, "tv", h) - 1)
                        transposes(B5, vt, tv_done, vt)
                        pe.wait_ge(kj_made, nth(t, 6 * H, 6 * h + 5))
                        pe.wait_ge(b4_read, b4_done(t, "tk", h) - 1)
                        transposes(B4, kj4[:].rearrange("p g j n -> p (g j n)"), tk_done, e4)
                    if s == base + 7:
                        pe.wait_ge(q_made, nth(t, 3 * H, 3 * h + 1))
                        pe.wait_ge(k_made, nth(t, 2 * H, 2 * h + 1))
                        pe.wait_ge(b4_read, b4_done(t, "scores", h) - 1)
                        for g in range(NG):
                            c = slice(g * P, (g + 1) * P)
                            pe.matmul(B4[:, c], e2[:, c], e1[:, c], start=True, stop=True)
                            for j in range(1, 4):
                                k = (None, e4[:, g * P:g * P + CHUNK], kj2[:, g].rearrange("p j n -> p (j n)"),
                                     kj3[:, g].rearrange("p j n -> p (j n)"))[j]
                                c = slice(g * P + j * CHUNK, g * P + (j + 1) * CHUNK)
                                pe.matmul(B4[0:j * CHUNK, c], k, q2[h % 2][:, c], start=True, stop=True)
                        pe.matmul(B4[0:SAMPLE, PT:T], e2[:, PT:T], e1[:, PT:T], start=True,
                                  stop=True).then_inc(sc_done, 1)
                        pe.wait_ge(b5_read, b5_done(t, "tv", h))
                        if h:
                            pe.wait_ge(s_made, s_value(t, last, h - 1, NG + NB - 1 if last else 3))
                        else:
                            pe.wait_ge(ybm_made, t * G)
                        for g in range(NG):
                            mm = pe.matmul(B6[:, g * P:(g + 1) * P], ktm[:, g, :], vtm[:, g, :], start=True, stop=True)
                        if not last:
                            mm = pe.matmul(B6[:, 3 * P:4 * P], ktm[0:CHUNK, 3, :], vtm[0:CHUNK, 3, :], start=True,
                                           stop=True)
                        mm.then_inc(p_done, 1)
                        if last:
                            pe.wait_ge(vms_made, 2 * h + 1)
                            sample_products(B7, vms[0])
                    if s == base + 8 and last:
                        pe.wait_ge(s_made, s_value(t, last, h, NG - 1))
                        pe.wait_ge(vms_made, 2 * h + 2)
                        sample_products(B6, vms[1])
                    if s == base + 9:
                        outputs(t, last, h)
                if s in MIX_SLOT:
                    g = MIX_SLOT[s]
                    pe.wait_ge(pooled_made, pooled_value(t, last, g))
                    if g < 2:
                        pe.wait_ge(s_made, s_value(t, last, H - 1, NG + NB - 1 if last else 3))
                    else:
                        pe.wait_ge(ybm_made, nth(t, G, g - 2))
                    pe.matmul((B6, B7)[g % 2][:, 0:T], wpl[:, g, :], pooled[g % 2][:], start=True,
                              stop=True).then_inc(mix_done, 1)
                if s == XNORM and not last:
                    pe.wait_ge(b4_read, b4_done(t, "xssq", 0) - 1)
                    pe.wait_ge(xacc_made, nth(t, KD - 1, KD - 2))
                    pe.matmul(B4[:, 0:T], ones[:], xacc[:], start=True, stop=True).then_inc(xssq_done, 1)
                if s == YNORM and not first(t):
                    y_squares(t - 1)

            def transposes(bank, src, done, rest):
                for g in range(NG):
                    pe.transpose(bank[:, g * P:(g + 1) * P], src[:, g * P:(g + 1) * P], ident[:])
                pe.transpose(bank[0:SAMPLE, 3 * P:4 * P], rest[:, PT:T], ident[:]).then_inc(done, 1)

            def sample_products(bank, v):
                pe.matmul(bank[:], ktm[0:SAMPLE, 3, :], v[0:SAMPLE], start=True, stop=True).then_inc(p_done, 1)

            def y_squares(t):
                pe.wait_ge(yacc_made, nth(t, KD - 1, KD - 2))
                pe.wait_ge(b5_read, b5_done(t, "yssq", 0) - 1)
                pe.matmul(B5[:, 0:T], ones[:], yacc[:], start=True, stop=True).then_inc(yssq_done, 1)

            def outputs(t, last, h):
                pe.wait_ge(b4_read, b4_done(t, "scores", h))
                pe.wait_ge(b5_read, b5_done(t, "o", h) - 1)
                for g in range(3):
                    c = slice(g * P, (g + 1) * P)
                    pe.matmul(B5[:, c], vtm[:, g, :], at_sb[:, c], start=(g == 0), stop=False,
                              skip_group_check=True)
                a3 = ats[0:SAMPLE, :] if last else at_sb[0:SAMPLE, PT:T]
                pe.matmul(B5[:, PT:T], vtm[0:SAMPLE, 3, :], a3, start=False, stop=False,
                          skip_group_check=True)
                pe.wait_ge(s_made, s_value(t, last, h, NG - 1))
                pe.wait_ge(s0_copied, nth(t, H, h))
                pe.wait_ge(q_made, nth(t, 3 * H, 3 * h + 2))
                for g in range(NG):
                    pe.matmul(B5[:, g * P:(g + 1) * P], s_all[:, g, :],
                              q4[h % 2][:, g].rearrange("p j n -> p (j n)"), start=False, stop=False,
                              skip_group_check=True)
                if not last:
                    mm = pe.matmul(B5[:, PT:T], s_all[:, 3, :], q2[h % 2][:, PT:T], start=False, stop=True,
                                   skip_group_check=True)
                if last:
                    pe.wait_ge(s0_landed[h % 2], 16 * (h // 2 + 1))
                    for b in range(NB):
                        c = PT + b * NT
                        mm = pe.matmul(B5[:, c:c + NT], s0[h % 2][:, b, :], q2[h % 2][:, c:c + NT],
                                       start=False, stop=(b == NB - 1), skip_group_check=True)
                mm.then_inc(o_done, 1)

            def product(t, s, acc, blocks):
                opened(t, acc)
                out = Z[ACC[acc] % NZ][:, 0:T]
                for i, (k, hi, lo, ready, value) in enumerate(blocks):
                    if ready is not None:
                        pe.wait_ge(ready, value)
                    mm = part(s, out, k, hi, lo, i == 0, i == len(blocks) - 1)
                mm.then_inc(acc_done, 1)

            def opened(t, acc):
                n = ACC[acc]
                pe.wait_ge(z_read[n % NZ], t * (NA // NZ) + n // NZ)

            def part(s, out, k, hi, lo, first, final):
                c = slice(k * P, (k + 1) * P)
                return three(out, (whi[s % RING][:, c], wlo[s % RING][:, c]), (hi[:], lo[:]), first, final)

            def tile(t, last):
                for s, (kind, i) in enumerate(UNITS):
                    small(t, last, s)
                    pe.wait_ge(wlo_made, nth(t, NU, s))
                    if kind == "y":
                        def ready(k):
                            return (ylo_made, nth(t, 8, Y_ORDER.index(k))) if i == 0 else (None, None)
                        product(t, s, ("ya", i), [(k, yhi[k], ylo[k], *ready(k)) for k in range(4)])
                        product(t, s, ("yb", i), [(k, yhi[k], ylo[k], *ready(k)) for k in range(4, 8)])
                    elif kind == "out" and i < 2:
                        if i == 0:
                            pe.wait_ge(wlo_made, nth(t, NU, s + 1))
                            for u in range(2):
                                opened(t, ("out", u))
                                for k in range(KD - 1):
                                    if u == 0:
                                        pe.wait_ge(mlo_made, nth(t, KD, k))
                                    part(s + u, Z[ACC[("out", u)] % NZ][:, 0:T], k, mhi[k], mlo[k], k == 0, False)
                            pe.wait_ge(mlo_made, nth(t, KD, KD - 1))
                            for u in range(2):
                                part(s + u, Z[ACC[("out", u)] % NZ][:, 0:T], KD - 1, mhi[KD - 1], mlo[KD - 1], False,
                                     True).then_inc(acc_done, 1)
                    elif kind == "out":
                        product(t, s, (kind, i), [(k, mhi[k], mlo[k], None, None) for k in range(KD)])
                    else:
                        product(t, s, (kind, i), [
                            (k, hhi[k], hlo[k], *((hlo_made, nth(t, KD, k)) if s == 0 else (None, None)))
                            for k in range(KD)])
                if last:
                    y_squares(t)

            pe.wait_ge(masks, MASKS)
            pe.wait_ge(zeroed, ZEROED)
            pe.wait_ge(cst_landed, 32)
            for k in range(KD):
                pe.wait_ge(xsq_made, k + 1)
                mm = pe.matmul(B4[:, 0:T], ones[:], psq[k][:], start=(k == 0), stop=(k == KD - 1))
            mm.then_inc(xssq_done, 1)
            tile(0, False)
            with pe.Fori(1, TILES - 1) as t:
                tile(t, False)
            tile(TILES - 1, True)

        @block.scalar
        def _(act):
            def split(t, s_or_n):
                n = s_or_n
                act.wait_ge(w_landed[n % RAW], landed(t, n))
                act.activation(whi[n % RING][:], wraw[n % RAW][:], ACT.Copy).then_inc(whi_made, 1)

            def x_square(t, k):
                if k == 0:
                    act.wait_ge(xin_landed, 16 * t + 16)
                if k >= 3:
                    act.wait_ge(xacc_made, nth(t, KD - 1, k - 3))
                act.activation(xacc[:] if k == 0 else xsq[k % 2][:], xin[:, k, :],
                               ACT.Square).then_inc(xsq_made, 1)

            def x_norm(value):
                act.preload_act_table_set(LN_EXP)
                act.wait_ge(xssq_done, value)
                act.activation(xrs[:], B4[:, 0:T], ACT.Ln, bias=eps_t[:], scale=1.0 / D).then_inc(b4_read, 1)

            def x_norm_exp(value, b4_value):
                act.wait_ge(b4_read, b4_value)
                act.activation(xrs[:], xrs[:], ACT.Exp, scale=-0.5).then_inc(xrs_made, 1)

            def h_hi(value, k):
                act.wait_ge(h32_made, (value - 1) * KD + k + 1)
                act.activation(hhi[k][:], h32[k % 2][:], ACT.Copy).then_inc(hhi_made, 1)

            def sigmoid(t, kind, i, out, done):
                act.wait_ge(acc_done, acc_ready(t, kind, i))
                act.activation(out[:], z_bank(kind, i)[:, 0:T], ACT.Sigmoid).then_inc(done, 1)

            def decays(t, last, h):
                act.wait_ge(z_sem("f", h), z_done(t, "f", h))
                act.activation(logf[:], sf[h % 2][:], ACT.Ln, bias=lb0[:, h:h + 1],
                               scale=oml[:, h:h + 1]).then_inc(logf_made, 1)
                act.wait_ge(b_made, nth(t, H, h))
                act.activation(e3[h % 2][:], bc[:], ACT.Exp).then_inc(exp_made, 1)
                act.wait_ge(d_made, nth(t, 2 * H, 2 * h))
                act.activation(e1[:], dd[:], ACT.Exp).then_inc(exp_made, 1)
                act.activation(e2[:], dd[:], ACT.Exp, scale=-1.0).then_inc(exp_made, 1)
                act.wait_ge(d_made, nth(t, 2 * H, 2 * h + 1))
                act.activation(e4[:], dl[:], ACT.Exp).then_inc(exp_made, 1)

            def head_norm(t, h):
                act.wait_ge(ssq_done, nth(t, H, h))
                act.activation(rst[:], B4[:, 0:T], ACT.Ln, bias=eps_t[:], scale=1.0 / P).then_inc(b4_read, 1)
                act.wait_ge(b4_read, b4_done(t, "ssq", h))
                act.activation(rst[:], rst[:], ACT.Exp, scale=-0.5).then_inc(rst_made, 1)

            def tile(t, last):
                for s in range(NU):
                    if s + AHEAD < NU or not last:
                        act.wait_ge(acc_done, t * NA + (LAST_ACC[s - 1] + 1 if s else 0))
                        split(t, s + AHEAD)
                    if s == 0 and not first(t):
                        y_square(t - 1, KD - 1)
                    if s == YNORM and not first(t):
                        y_norm(t - 1)
                    for h in range(H):
                        if s == 4 * h + 1:
                            sigmoid(t, "f", h, sf[h % 2], z_sem("f", h))
                        if s == 4 * h + 2:
                            sigmoid(t, "q", h, qf[h % 2], sq_made)
                        if s == 4 * h + 3:
                            act.wait_ge(acc_done, acc_ready(t, "i", h))
                            act.activation(vt[:], z_bank("i", h)[:, 0:T], ACT.Copy).then_inc(z_sem("i", h), 1)
                        if s == 4 * h + 4:
                            sigmoid(t, "g", h, ga[h % 3], sg_made)
                        if s == 4 * h + 6:
                            act.wait_ge(tv_done, nth(t, H, h))
                            act.activation(vtm[:, 0:3, :], B5[:, 0:3 * P].rearrange("p (g v) -> p g v", v=P), ACT.Copy)
                            act.activation(vtm[0:SAMPLE, 3, :], B5[0:SAMPLE, 3 * P:4 * P],
                                           ACT.Copy).then_inc(b5_read, 1)
                        if s == 4 * h + 9:
                            act.wait_ge(o_done, nth(t, H, h))
                            act.activation(osq[:], B5[:, 0:T], ACT.Square).then_inc(osq_made, 1)
                            act.activation(o_sb[:], B5[:, 0:T], ACT.Copy).then_inc(b5_read, 1)
                        if s == 4 * h + 13:
                            act.wait_ge(og_made, nth(t, H, h))
                            act.activation(yhi[h][:], og[h % 2][:], ACT.Copy).then_inc(yhi_made, 1)
                    if s % 4 == 0 and 4 <= s <= 24:
                        act.preload_act_table_set(LN_EXP)
                        if s <= 16:
                            decays(t, last, s // 4 - 1)
                        if s >= 12:
                            head_norm(t, s // 4 - 3)
                    for g in range(G):
                        if s == 17 + 2 * g:
                            act.wait_ge(acc_done, acc_ready(t, "u", g))
                            act.wait_ge(hist_kept, t * G)
                            z = z_bank("u", g)
                            if last:
                                act.activation(ext[:, g, BUF:BUF + PT], z[:, 0:PT], ACT.Copy)
                                act.activation(exts[:, g, :, BUF:BUF + NT],
                                               z[:, PT:T].rearrange("p (b n) -> p b n", n=NT),
                                               ACT.Copy).then_inc(z_sem("u", g), 1)
                            else:
                                act.activation(ext[:, g, BUF:EXT], z[:, 0:T], ACT.Copy).then_inc(z_sem("u", g), 1)
                        if s == 18 + 2 * g:
                            if g == 3:
                                act.wait_ge(ylo_made, nth(t, 8, Y_ORDER.index(4)))
                            sigmoid(t, "b", g, bg[g % 3], sb_made)
                    if s in MIX_SLOT:
                        g = MIX_SLOT[s]
                        act.wait_ge(ybm_made, nth(t, G, g))
                        act.activation(yhi[4 + g][:], bg[g % 3][:], ACT.Copy).then_inc(yhi_made, 1)
                    kind, j = UNITS[s - 1] if s else (None, 0)
                    if kind == "ma":
                        sigmoid(t, "ma", j, gA[j % 3], z_sem("ma", j))
                    if kind == "mb":
                        sigmoid(t, "mb", j, gB[j % 3], z_sem("mb", j))
                    if s in XSQ_SLOT and not last:
                        x_square(t, XSQ_SLOT[s])
                    if s == XNORM and not last:
                        x_norm(t + 2)
                        x_norm_exp(t + 2, b4_done(t, "xssq", 0))
                    if kind == "y":
                        act.wait_ge(merged, nth(t, KD, j))
                        act.activation(mhi[j][:], mA[j % 2][:], ACT.Copy).then_inc(mhi_made, 1)
                    if s in H_SLOT and not last:
                        h_hi(t + 2, H_SLOT[s])
                    if kind == "out":
                        y_square(t, j)
                if last:
                    y_square(t, KD - 1)
                    y_norm(t)

            def y_norm(t):
                act.preload_act_table_set(LN_EXP)
                act.wait_ge(yssq_done, t + 1)
                act.activation(yrs[:], B5[:, 0:T], ACT.Ln, bias=eps_t[:], scale=1.0 / D).then_inc(b5_read, 1)
                act.wait_ge(b5_read, b5_done(t, "yssq", 0))
                act.activation(yrs[:], yrs[:], ACT.Exp, scale=-0.5).then_inc(yrs_made, 1)

            def y_square(t, j):
                act.wait_ge(z_sem("out", j), z_done(t, "out", j))
                if j >= 3:
                    act.wait_ge(yacc_made, nth(t, KD - 1, j - 3))
                act.activation(yacc[:] if j == 0 else ysq[j % 2][:], xres[:, j, :], ACT.Square).then_inc(ysq_made, 1)

            act.preload_act_table_set(LN_EXP)
            act.wait_ge(zeroed, ZEROED)
            for k in range(KD):
                act.wait_ge(x0_landed[k // 2], 16)
                act.activation(psq[k][:], xin[:, k, :], ACT.Square).then_inc(xsq_made, 1)
            for n in range(RAW):
                split(0, n)
            act.wait_ge(lb_made, 3)
            act.activation(lb[:, 3:5], lb[:, 3:5], ACT.Exp).then_inc(lbe_made, 1)
            x_norm(1)
            x_norm_exp(1, 1)
            for n in range(RAW, AHEAD):
                split(0, n)
            for k in range(KD):
                h_hi(1, k)
            act.wait_ge(lb_made, LB_STEPS)
            tile(0, False)
            with act.Fori(1, TILES - 1) as t:
                tile(t, False)
            tile(TILES - 1, True)

        @block.vector
        def _(dve):
            def split(t, n):
                dve.wait_ge(whi_made, nth(t, NU, n))
                dve.tensor_tensor(wlo[n % RING][:], wraw[n % RAW][:], whi[n % RING][:].bitcast(F32),
                                  ALU.subtract).then_inc(wlo_made, 1)

            def h_block(value, k):
                if k == 0:
                    dve.wait_ge(xrs_made, value)
                if 2 <= k < KD:
                    dve.wait_ge(hlo_made, (value - 1) * KD + k - 1)
                if k < KD:
                    dve.scalar_tensor_tensor(out=h32[k % 2][:], in0=xin[:, k, :],
                                             scalar=cst[:, C_NG + k:C_NG + k + 1], in1=xrs[:], op0=ALU.mult,
                                             op1=ALU.mult).then_inc(h32_made, 1)
                if k:
                    dve.wait_ge(hhi_made, (value - 1) * KD + k)
                    dve.tensor_tensor(hlo[k - 1][:], h32[(k - 1) % 2][:], hhi[k - 1][:].bitcast(F32),
                                      ALU.subtract).then_inc(hlo_made, 1)

            def gated(t, kind, i, out, made, scalar):
                dve.wait_ge(made, nth(t, 4, i))
                dve.scalar_tensor_tensor(out=out[:], in0=z_bank(kind, i)[:, 0:T], scalar=scalar, in1=out[:],
                                         op0=ALU.mult, op1=ALU.mult).then_inc(z_sem(kind, i), 1)

            def sums(t, last, h):
                dve.wait_ge(logf_made, nth(t, H, h))
                parts = [(0, PT, CHUNK, smask[:, 0:PT]), (PT, T, NT, smask_s[:])] if last else [(0, T, CHUNK, smask[:])]
                for lo, hi, n, mask in parts:
                    ins = dve.tensor_tensor_scan(bc[:, lo:hi], mask, logf[:, lo:hi], 0.0, ALU.mult, ALU.add)
                ins.then_inc(b_made, 1)
                dve.wait_ge(b_made, nth(t, H, h))
                for out, at, sign in ((dd, 0, 1), (dl, 1, -1)):
                    for lo, hi, n, _ in parts:
                        v = bc[:, lo:hi].rearrange("p (c n) -> p c n", n=n)
                        m = n // 2 if at == 0 else n - 1
                        r = v[:, :, m:m + 1].broadcast_to([P, (hi - lo) // n, n])
                        o = out[:, lo:hi].rearrange("p (c n) -> p c n", n=n)
                        a, b = (v, r) if sign == 1 else (r, v)
                        ins = dve.tensor_tensor(o, a, b, ALU.subtract)
                    ins.then_inc(d_made, 1)
                dve.wait_ge(z_sem("q", h), z_done(t, "q", h))
                dve.wait_ge(exp_made, nth(t, 4 * H, 4 * h))
                dve.tensor_tensor(q2[h % 2][:], qf[h % 2][:], e3[h % 2][:], ALU.mult).then_inc(q_made, 1)
                dve.wait_ge(exp_made, nth(t, 4 * H, 4 * h + 1))
                dve.tensor_tensor(e1[:], qf[h % 2][:], e1[:], ALU.mult).then_inc(q_made, 1)
                dve.tensor_copy(dprev[:, :, 1:4], chunk_decay(h)[:, :, 0:3]).then_inc(dq_made, 1)
                dve.wait_ge(dq_made, nth(t, 3 * H, 3 * h))
                dve.tensor_tensor_scan(dq[:].rearrange("p g j -> p (g j)"), dprev[:].rearrange("p g j -> p (g j)"),
                                       dfirst[:].rearrange("p g j -> p (g j)"), 0.0, ALU.mult,
                                       ALU.add).then_inc(dq_made, 1)
                dve.wait_ge(dq_made, nth(t, 3 * H, 3 * h + 1))
                dve.tensor_tensor(dg[:], dq[:, :, 3], chunk_decay(h)[:, :, 3], ALU.mult).then_inc(dq_made, 1)
                dve.wait_ge(q_made, nth(t, 3 * H, 3 * h))
                dve.tensor_tensor(q4[h % 2][:].rearrange("p g j n -> p (g j) n"),
                                  q2[h % 2][:, 0:PT].rearrange("p (c n) -> p c n", n=CHUNK),
                                  dq[:].rearrange("p g j -> p (g j)").unsqueeze(2).broadcast_to([P, 4 * NG, CHUNK]),
                                  ALU.mult).then_inc(q_made, 1)

            def chunk_decay(h):
                return e3[h % 2][:, 0:PT].rearrange("p (g j n) -> p g j n", g=NG, n=CHUNK)[:, :, :, CHUNK - 1]

            def decayed_keys(t, h):
                dve.wait_ge(k_made, nth(t, 2 * H, 2 * h + 1))
                k2 = e4[:, 0:PT].rearrange("p (g j n) -> p g j n", g=NG, n=CHUNK)
                src = k2[:, :, 0:1, :]
                for j, out in ((1, kj2), (2, kj3), (3, kj4)):
                    d = chunk_decay(h)[:, :, j:j + 1]
                    if j > 1:
                        dve.wait_ge(kj_made, nth(t, 6 * H, 6 * h + 2 * j - 3))
                    dve.tensor_tensor(out[:, :, 0:j, :].rearrange("p g j n -> p g (j n)"),
                                      src.rearrange("p g j n -> p g (j n)"),
                                      d.broadcast_to([P, NG, j * CHUNK]), ALU.mult).then_inc(kj_made, 1)
                    dve.tensor_copy(out[:, :, j, :], k2[:, :, j, :]).then_inc(kj_made, 1)
                    src = out[:]

            def update(t, last, h, g):
                if g == 0:
                    dve.wait_ge(p_done, p_value(t, last, h, 0))
                else:
                    dve.wait_ge(s_made, s_value(t, last, h, g - 1))
                s_in = s_all[:, g, :] if g else carry[:, h, :]
                s_out = carry[:, h, :] if g == (NG - 1 if last else NG) else s_all[:, g + 1, :]
                decay = dg[:, g:g + 1] if g < NG else e3[h % 2][:, T - 1:T]
                dve.scalar_tensor_tensor(out=s_out, in0=s_in, scalar=decay, in1=B6[:, g * P:(g + 1) * P],
                                         op0=ALU.mult, op1=ALU.add).then_inc(s_made, 1)

            def sample_update(t, h, b):
                if b % 4 == 0:
                    dve.wait_ge(p_done, p_value(t, True, h, 1 + b // 4))
                if b == 0:
                    dve.wait_ge(s0_landed[h % 2], 16 * (h // 2 + 1))
                    if h:
                        dve.wait_ge(snew_stored, 16 * h)
                e = PT + b * NT + NT - 1
                dve.scalar_tensor_tensor(out=snew[:, b, :], in0=s0[h % 2][:, b, :], scalar=e3[h % 2][:, e:e + 1],
                                         in1=(B7, B6)[b // 4][:, (b % 4) * P:(b % 4 + 1) * P], op0=ALU.mult,
                                         op1=ALU.add).then_inc(s_made, 1)

            def means(t, last, g):
                w = WINDOWS[g]
                src, srcs = (pb, pbs) if g % 2 else (pa, pas)
                n = PT if last else T
                dve.wait_ge(win_made, win_value(t, last, g, g, last))
                if g == 0:
                    dve.wait_ge(rc_used, RC_FIRST + t)
                if g >= 2:
                    dve.wait_ge(mix_done, nth(t, G, g - 2))
                dve.tensor_tensor(ptmp[:], src[:, BUF:2 * BUF], rc[:, g, :], ALU.mult).then_inc(ptmp_made, 1)
                dve.scalar_tensor_tensor(out=pooled[g % 2][:, BUF:n], in0=src[:, 2 * BUF:BUF + n], scalar=1.0 / w,
                                         in1=ext[:, g, 2 * BUF:BUF + n], op0=ALU.mult, op1=ALU.subtract)
                if last:
                    dve.scalar_tensor_tensor(
                        out=pooled[g % 2][:, PT:T].rearrange("p (b n) -> p b n", n=NT), in0=srcs[:, :, BUF:BUF + NT],
                        scalar=1.0 / w, in1=exts[:, g, :, BUF:BUF + NT], op0=ALU.mult, op1=ALU.subtract)
                dve.wait_ge(ptmp_made, nth(t, G, g))
                dve.tensor_tensor(pooled[g % 2][:, 0:BUF], ptmp[:], ext[:, g, BUF:2 * BUF],
                                  ALU.subtract).then_inc(pooled_made, 1)
                if not last:
                    dve.wait_ge(pooled_made, nth(t, G, g))
                    dve.tensor_copy(ext[:, g, 0:BUF], ext[:, g, T:T + BUF]).then_inc(hist_kept, 1)

            def merge(t, j):
                for acc, gate, out, n in (("ya", gA, mA, 0), ("yb", gB, mB, 1)):
                    dve.wait_ge(acc_done, acc_ready(t, acc, j))
                    dve.wait_ge(z_sem("m" + acc[1], j), z_done(t, "m" + acc[1], j))
                    dve.tensor_tensor(out[j % 2][:], z_bank(acc, j)[:, 0:T], gate[j % 3][:],
                                      ALU.mult).then_inc(z_sem(acc, j), 1)
                dve.wait_ge(mhi_made, nth(t, KD, j))
                dve.tensor_tensor(mlo[j][:], mA[j % 2][:], mhi[j][:].bitcast(F32), ALU.subtract).then_inc(mlo_made, 1)

            def residual(t, j):
                if j == 0:
                    dve.wait_ge(xres_landed, 16 * t + 16)
                dve.wait_ge(acc_done, acc_ready(t, "out", j))
                dve.tensor_tensor(xres[:, j, :], z_bank("out", j)[:, 0:T], xres[:, j, :],
                                  ALU.add).then_inc(z_sem("out", j), 1)

            def tile(t, last):
                for s in range(NU):
                    if s + AHEAD < NU or not last:
                        split(t, s + AHEAD)
                    if s == 0 and not first(t):
                        residual(t - 1, KD - 1)
                    if s == YNORM and not first(t):
                        output(t - 1)
                    for h in range(H):
                        if s == 4 * h + 1:
                            dve.wait_ge(z_sem("f", h), z_done(t, "f", h))
                            dve.tensor_scalar(kin[h % 2][:], sf[h % 2][:], noml[:, h:h + 1], oml[:, h:h + 1],
                                              ALU.mult, ALU.add).then_inc(kin_made, 1)
                        if s == 4 * h + 2:
                            gated(t, "q", h, qf[h % 2], sq_made, QSCALE)
                        if s == 4 * h + 4:
                            gated(t, "g", h, ga[h % 3], sg_made, cst[:, C_GN:C_GN + 1])
                            sums(t, last, h)
                        if s == 4 * h + 5:
                            decayed_keys(t, h)
                        if s == 4 * h + 6:
                            dve.wait_ge(tk_done, nth(t, H, h))
                            dve.tensor_copy(ktm[:, 0:3, :], B4[:, 0:3 * P].rearrange("p (g v) -> p g v", v=P))
                            dve.tensor_copy(ktm[0:SAMPLE, 3, :], B4[0:SAMPLE, 3 * P:4 * P]).then_inc(b4_read, 1)
                            if last:
                                dve.wait_ge(b5_read, b5_done(t, "tv", h))
                                for half in range(2):
                                    dve.tensor_tensor(
                                        vms[half][0:SAMPLE], vtm[0:SAMPLE, 3:4, :].broadcast_to([SAMPLE, 4, P]),
                                        bmask[0:SAMPLE, 4 * half:4 * half + 4].unsqueeze(2).broadcast_to([SAMPLE, 4, P]),
                                        ALU.mult).then_inc(vms_made, 1)
                        if s == 4 * h + 7:
                            dve.wait_ge(sc_done, nth(t, H, h))
                            dve.wait_ge(o_done, t * H + h)
                            if h == 0:
                                dve.wait_ge(s_made, t * H * 4)
                            dve.tensor_copy(s_all[:, 0, :], carry[:, h, :]).then_inc(s0_copied, 1)
                            dve.copy_predicated(at_sb[:, 0:PT], cmask[:].bitcast(U32).rearrange("p a b -> p (a b)"),
                                                B4[:, 0:PT])
                            out3, mask3 = (ats[0:SAMPLE, :], cmask_s[0:SAMPLE]) if last else (
                                at_sb[0:SAMPLE, PT:T], cmask[0:SAMPLE, 0:1, 0:SAMPLE])
                            dve.copy_predicated(out3, mask3.bitcast(U32).rearrange("p a b -> p (a b)"),
                                                B4[0:SAMPLE, PT:T]).then_inc(b4_read, 1)
                            for g in range(NG if last else 4):
                                update(t, last, h, g)
                            if last:
                                for b in range(4):
                                    sample_update(t, h, b)
                        if s == 4 * h + 8 and last:
                            for b in range(4, NB):
                                sample_update(t, h, b)
                        if s == 4 * h + 13:
                            dve.wait_ge(yhi_made, nth(t, 8, Y_ORDER.index(h)))
                            dve.tensor_tensor(ylo[h][:], og[h % 2][:], yhi[h][:].bitcast(F32),
                                              ALU.subtract).then_inc(ylo_made, 1)
                    if s % 4 == 0 and 12 <= s <= 24:
                        h = s // 4 - 3
                        dve.wait_ge(b5_read, b5_done(t, "o", h))
                        dve.wait_ge(rst_made, nth(t, H, h))
                        dve.tensor_tensor(og[h % 2][:], o_sb[:], rst[:], ALU.mult).then_inc(t1_made, 1)
                        dve.wait_ge(t1_made, nth(t, H, h))
                        dve.tensor_tensor(og[h % 2][:], og[h % 2][:], ga[h % 3][:], ALU.mult).then_inc(og_made, 1)
                    for g in range(G):
                        if s == 18 + 2 * g:
                            gated(t, "b", g, bg[g % 3], sb_made, cst[:, C_PS + g:C_PS + g + 1])
                        if s == 18 + 2 * g:
                            means(t, last, g)
                    if s in MIX_SLOT:
                        g = MIX_SLOT[s]
                        dve.wait_ge(mix_done, nth(t, G, g))
                        dve.wait_ge(z_sem("b", g), z_done(t, "b", g))
                        dve.tensor_tensor(bg[g % 3][:], (B6, B7)[g % 2][:, 0:T], bg[g % 3][:],
                                          ALU.mult).then_inc(ybm_made, 1)
                        dve.wait_ge(yhi_made, nth(t, 8, Y_ORDER.index(4 + g)))
                        dve.tensor_tensor(ylo[4 + g][:], bg[g % 3][:], yhi[4 + g][:].bitcast(F32),
                                          ALU.subtract).then_inc(ylo_made, 1)
                    kind, j = UNITS[s - 1] if s else (None, 0)
                    if kind == "y":
                        merge(t, j)
                    if kind == "out":
                        residual(t, j)
                    if s in H_SLOT and not last:
                        h_block(t + 2, H_SLOT[s])
                        if H_SLOT[s] == KD - 1:
                            h_block(t + 2, KD)
                    if s == 27 and not last:
                        for g in range(G):
                            ins = dve.memset(rc[:, g, :], 1.0 / WINDOWS[g])
                        ins.then_inc(rc_used, 1)
                if last:
                    residual(t, KD - 1)
                    output(t)

            def output(t):
                dve.wait_ge(yrs_made, t + 1)
                for j in range(KD):
                    dve.scalar_tensor_tensor(out=xres[:, j, :], in0=xres[:, j, :],
                                             scalar=cst[:, C_FG + j:C_FG + j + 1], in1=yrs[:], op0=ALU.mult,
                                             op1=ALU.mult).then_inc(y_made, 1)

            zero = [ext[:, :, 0:BUF], carry[:], at_sb[:], ats[:], dprev[:]]
            for z in zero:
                dve.memset(z, 0.0).then_inc(zeroed, 1)
            dve.memset(eps_t[:], EPS).then_inc(zeroed, 1)

            for n in range(RAW):
                split(0, n)
            dve.wait_ge(cst_landed, 32)
            l0, l1 = cst[:, C_LB:C_LB + H], cst[:, C_LB + H:C_LB + 2 * H]
            dve.tensor_tensor(lb[:, 5], l0, l1, ALU.max).then_inc(lb_made, 1)
            dve.wait_ge(lb_made, 1)
            dve.tensor_tensor(lb[:, 3], l0, lb[:, 5], ALU.subtract).then_inc(lb_made, 1)
            dve.tensor_tensor(lb[:, 4], l1, lb[:, 5], ALU.subtract).then_inc(lb_made, 1)
            dve.wait_ge(lbe_made, 1)
            dve.tensor_tensor(lb[:, 6], lb[:, 3], lb[:, 4], ALU.add).then_inc(lb_made, 1)
            dve.wait_ge(lb_made, 4)
            dve.reciprocal(lb[:, 7], lb[:, 6]).then_inc(lb_made, 1)
            dve.wait_ge(lb_made, 5)
            dve.tensor_tensor(lb[:, 0], lb[:, 3], lb[:, 7], ALU.mult).then_inc(lb_made, 1)
            dve.wait_ge(lb_made, 6)
            dve.tensor_scalar(lb[:, 1], lb[:, 0], -1.0, 1.0, ALU.mult, ALU.add).then_inc(lb_made, 1)
            dve.wait_ge(lb_made, 7)
            dve.tensor_scalar(lb[:, 2], lb[:, 1], -1.0, None, ALU.mult).then_inc(lb_made, 1)
            dve.wait_ge(masks, MASKS)
            for g in range(G):
                dve.tensor_scalar(rc[:, g, :], rc[:, g, :], float(WINDOWS[g]), None, ALU.min).then_inc(rc_used, 1)
            dve.wait_ge(rc_used, G)
            dve.reciprocal(rc[:], rc[:]).then_inc(rc_used, 1)
            for n in range(RAW, AHEAD):
                split(0, n)
            for k in range(KD + 1):
                h_block(1, k)
            dve.wait_ge(lb_made, LB_STEPS)
            tile(0, False)
            with dve.Fori(1, TILES - 1) as t:
                tile(t, False)
            tile(TILES - 1, True)

        @block.gpsimd
        def _(pool):
            count = [0]

            def step(ins):
                ins.then_inc(masks, 1)
                count[0] += 1
                pool.wait_ge(masks, count[0])

            def x_sum(t, k):
                pool.wait_ge(xsq_made, (t + 1) * KD + k + 1)
                if k > 1:
                    pool.wait_ge(xacc_made, nth(t, KD - 1, k - 2))
                pool.tensor_tensor(xacc[:], xacc[:], xsq[k % 2][:], ALU.add).then_inc(xacc_made, 1)

            def y_sum(t, j):
                pool.wait_ge(ysq_made, nth(t, KD, j))
                if j > 1:
                    pool.wait_ge(yacc_made, nth(t, KD - 1, j - 2))
                pool.tensor_tensor(yacc[:], yacc[:], ysq[j % 2][:], ALU.add).then_inc(yacc_made, 1)

            def wins(level):
                return lambda lo, hi: (pa, pb)[level % 2][:, lo:hi]

            def windows(t, last, g):
                pool.wait_ge(z_sem("u", g), z_done(t, "u", g))
                if g == 0 and last:
                    pool.wait_ge(buf_landed, 16)
                if g >= 1:
                    pool.wait_ge(pooled_made, pooled_value(t, last, g - 1))
                for level in range(g + 1):
                    w = 1 << level
                    n = PT if last else T
                    if level:
                        pool.wait_ge(win_made, win_value(t, last, g, level - 1, last))
                    first = 2 * w - 1
                    if level == 0:
                        a = ext[:, g, first:BUF + n]
                        b = ext[:, g, first - w:BUF + n - w]
                    else:
                        src = wins(level - 1)
                        a, b = src(first, BUF + n), src(first - w, BUF + n - w)
                    pool.tensor_tensor(wins(level)(first, BUF + n), a, b, ALU.add).then_inc(win_made, 1)
                    if last:
                        e = BUF + NT
                        if level == 0:
                            a, b = exts[:, g, :, first:e], exts[:, g, :, first - w:e - w]
                        else:
                            ss = (pas, pbs)[(level - 1) % 2]
                            a, b = ss[:, :, first:e], ss[:, :, first - w:e - w]
                        pool.tensor_tensor((pas, pbs)[level % 2][:, :, first:e], a, b, ALU.add).then_inc(win_made, 1)

            def tile(t, last):
                for s in range(NU):
                    if s == 0 and not first(t):
                        y_sum(t - 1, KD - 1)
                    for h in range(H):
                        if s == 4 * h + 4:
                            pool.wait_ge(kin_made, nth(t, H, h))
                            pool.wait_ge(exp_made, nth(t, 4 * H, 4 * h + 2))
                            pool.tensor_tensor(e2[:], kin[h % 2][:], e2[:], ALU.mult).then_inc(k_made, 1)
                            pool.wait_ge(exp_made, nth(t, 4 * H, 4 * h + 3))
                            pool.tensor_tensor(e4[:], kin[h % 2][:], e4[:], ALU.mult).then_inc(k_made, 1)
                    for g in range(G):
                        if s == 17 + 2 * g:
                            windows(t, last, g)
                    kind, j = UNITS[s - 1] if s else (None, 0)
                    if kind == "y":
                        pool.wait_ge(z_sem("yb", j), z_done(t, "yb", j))
                        pool.wait_ge(z_sem("ya", j), z_done(t, "ya", j))
                        pool.tensor_tensor(mA[j % 2][:], mA[j % 2][:], mB[j % 2][:], ALU.add).then_inc(merged, 1)
                    if s in XSQ_SLOT and not last and XSQ_SLOT[s]:
                        x_sum(t, XSQ_SLOT[s])
                    if kind == "out" and j:
                        y_sum(t, j)
                if last:
                    y_sum(t, KD - 1)

            for value, m in ((1.0, ones[:]), (0.0, ident[:]), (1.0, cmask[:]), (1.0, cmask_s[:]), (1.0, bmask[:]),
                             (1.0, smask[:]), (1.0, smask_s[:]), (0.0, dfirst[:])):
                step(pool.memset(m, value))
            step(pool.affine_select(out=ident[:], in_=ident[:], compare_op=ALU.not_equal, fill=1.0, base=0,
                                    pattern=[[-1, P]], channel_multiplier=1))
            step(pool.memset(dfirst[:, :, 0:1], 1.0))
            step(pool.memset(smask[:].rearrange("p (c n) -> p c n", n=CHUNK)[:, :, 0:1], 0.0))
            step(pool.memset(smask_s[:].rearrange("p (c n) -> p c n", n=NT)[:, :, 0:1], 0.0))
            step(pool.affine_select(out=cmask[:], in_=cmask[:], compare_op=ALU.is_ge, fill=0.0, base=0,
                                    pattern=[[0, NG], [1, P]], channel_multiplier=-1))
            m = cmask_s[:]
            step(pool.affine_select(out=m, in_=m, compare_op=ALU.is_ge, fill=0.0, base=0,
                                    pattern=[[NT, NB], [1, NT]], channel_multiplier=-1))
            step(pool.affine_select(out=m, in_=m, compare_op=ALU.is_ge, fill=0.0, base=0,
                                    pattern=[[-NT, NB], [0, NT]], channel_multiplier=1))
            step(pool.affine_select(out=bmask[:], in_=bmask[:], compare_op=ALU.is_ge, fill=0.0, base=0,
                                    pattern=[[-NT, NB]], channel_multiplier=1))
            step(pool.affine_select(out=bmask[:], in_=bmask[:], compare_op=ALU.is_ge, fill=0.0, base=NT - 1,
                                    pattern=[[NT, NB]], channel_multiplier=-1))
            step(pool.iota(rc[:], pattern=[[0, G], [1, BUF]], base=1, channel_multiplier=0,
                           allow_small_or_imprecise_dtypes=True))
            assert count[0] == MASKS
            tile(0, False)
            with pool.Fori(1, TILES - 1) as t:
                tile(t, False)
            tile(TILES - 1, True)


def column_block(w, c):
    k = w.shape[0] // P
    return w[:, c:c + P].reshape(k, P, P).transpose(1, 0, 2).reshape(P, k * P)


def kernel(x_prompt, x_sample, state_hgrn, state_pool, norm_g, w_in, lb_logits, hgrn_norm_g, w_proj_a, w_pool,
           pool_scale, w_proj_b, w_out, final_norm_g):
    import concourse.bacc as bacc
    from concourse.bass_utils import run_bass_kernel_spmd

    a = [np.asarray(v) for v in (x_prompt, x_sample, state_hgrn, state_pool, norm_g, w_in, lb_logits, hgrn_norm_g,
                                 w_proj_a, w_pool, pool_scale, w_proj_b, w_out, final_norm_g)]
    (xp, xs, sh, spl, ng, win, lbl, hn, wa, wp, psc, wb, wo, fg) = a
    win, wa, wb, wo = win[0], wa[0], wb[0], wo[0]
    x = np.concatenate([xp.reshape(SEQ, D), xs.reshape(SAMPLE, D)]).reshape(TILES, T, KD, P).transpose(0, 3, 2, 1)
    width = D // 2
    first = {"q": 0, "f": width, "i": 2 * width, "g": 3 * width, "u": 4 * width, "b": 5 * width,
             "ma": 6 * width, "mb": 6 * width + D}
    blocks = []
    for kind, i in UNITS:
        if kind == "y":
            blocks.append(np.concatenate([column_block(wa, i * P), column_block(wb, i * P)], axis=1))
        elif kind == "out":
            blocks.append(column_block(wo, i * P))
        else:
            blocks.append(column_block(win, first[kind] + i * P))
    consts = np.concatenate([ng.reshape(KD, P).T, hn.reshape(1, P).T, psc.reshape(G, P).T, fg.reshape(KD, P).T,
                             lbl.reshape(2, H, P).transpose(2, 0, 1).reshape(P, 2 * H)], axis=1)
    arrays = {
        "xT": x, "w_all": np.stack(blocks), "consts": consts, "w_pool": wp[0].transpose(1, 0, 2),
        "s_in": sh[0].transpose(1, 2, 0, 3), "buf_in": spl[0].reshape(NB, BUF, G, P).transpose(3, 2, 0, 1),
    }
    arrays = {n: np.ascontiguousarray(v) for n, v in arrays.items()}
    outs = {"yT": x.shape, "sp_out": (P, H, P), "pp_out": (P, G, BUF), "ss_out": (H, P, NB, P),
            "ps_out": (P, G, NB, BUF)}
    nc = bacc.Bacc("TRN2", target_bir_lowering=False, num_devices=1)
    args = [nc.dram_tensor(n, v.shape, mybir.dt.from_np(v.dtype), kind="ExternalInput").ap()
            for n, v in arrays.items()]
    args += [nc.dram_tensor(n, v, F32, kind="ExternalOutput").ap() for n, v in outs.items()]
    step_kernel(nc, *args)
    r = run_bass_kernel_spmd(nc, [arrays], core_ids=[0]).results[0]
    y = np.asarray(r["yT"]).transpose(0, 3, 2, 1).reshape(SEQ + SAMPLE, D)
    return (
        np.ascontiguousarray(y[:SEQ]).reshape(1, SEQ, D),
        np.ascontiguousarray(y[SEQ:]).reshape(NB, NT, D),
        np.ascontiguousarray(np.asarray(r["sp_out"]).transpose(1, 0, 2)).reshape(1, 1, H, P, P),
        np.ascontiguousarray(np.asarray(r["pp_out"]).transpose(2, 1, 0)).reshape(1, 1, BUF, G * P),
        np.ascontiguousarray(np.asarray(r["ss_out"]).transpose(2, 0, 1, 3)).reshape(1, NB, H, P, P),
        np.ascontiguousarray(np.asarray(r["ps_out"]).transpose(2, 3, 1, 0)).reshape(1, NB, BUF, G * P),
    )
```

```python
from contextlib import ExitStack

import numpy as np

import concourse.bass as bass
from concourse import mybir

F32 = mybir.dt.float32
F32R = mybir.dt.float32r
U32 = mybir.dt.uint32
ALU = mybir.AluOpType
ACT = mybir.ActivationFunctionType

P = 128
D = 1024
KD = D // P
SEQ = 2048
NB, NT = 8, 4
SAMPLE = NB * NT
T = 416
TILES = (SEQ + SAMPLE) // T
H = 4
G = 4
CHUNK = 32
NG = 3
PT = T - SAMPLE
BUF = 15
WINDOWS = (2, 4, 8, 16)
EPS = 1e-6
QSCALE = float(P) ** -0.5
RAW = 2
RING = 4
AHEAD = RING - 1

UNITS = [(kind, h) for h in range(H) for kind in "fqig"]
UNITS += [(kind, g) for g in range(G) for kind in "ub"]
UNITS += [("ma", 0), ("mb", 0)]
for _j in range(1, KD):
    UNITS += [("ma", _j), ("mb", _j), ("y", _j - 1)]
UNITS += [("y", KD - 1)]
UNITS += [("out", _j) for _j in range(KD)]
NU = len(UNITS)
SLOT = {u: s for s, u in enumerate(UNITS)}

ACCS = []
for _kind, _i in UNITS:
    ACCS += [("ya", _i), ("yb", _i)] if _kind == "y" else [(_kind, _i)]
NA = len(ACCS)
ACC = {a: n for n, a in enumerate(ACCS)}
NZ = 4
LAST_ACC = [ACC[("yb", i)] if kind == "y" else ACC[(kind, i)] for kind, i in UNITS]

MIX_SLOT = {22: 0, 23: 1, 25: 2, 26: 3}
MEANS_SPLIT = {19 + 2 * g: g for g in range(G)}
XSQ_SLOT = {28 + 2 * k: k for k in range(KD)}
XNORM = 46
H_SLOT = {47 + k: k for k in range(KD)}

B4_USES, B5_USES = [], []
for _s in range(NU):
    for _h in range(H):
        if _s == 4 * _h + 12:
            B4_USES.append(("ssq", _h))
        if _s == 4 * _h + 6:
            B5_USES.append(("tv", _h))
        if _s == 4 * _h + 7:
            B4_USES.append(("scores", _h))
        if _s == 4 * _h + 9:
            B5_USES.append(("o", _h))
    if _s == XNORM:
        B4_USES.append(("xssq", 0))
B5_USES.append(("yssq", 0))

C_NG, C_GN, C_PS, C_FG, C_LB = 0, 8, 9, 13, 21
C_N = 29

Y_ORDER = [k for _, k in sorted([(4 * h + 13, h) for h in range(H)]
                                + [(s + 0.5, 4 + g) for s, g in MIX_SLOT.items()])]
MASKS = 18
ZEROED = 7
LN_EXP = "natural_log_exp_and_others"
LB_STEPS = 8
KJ = 8
POOL_OUT = 3
RC_FIRST = G + 1
YNORM = 4


def step_kernel(nc, xT, w_all, consts, w_pool, s_in, buf_in, yT, sp_out, pp_out, ss_out, ps_out):
    with ExitStack() as ctx:
        start = (int(nc.sbuf_base) + 63) // 64 * 64
        top = [start]

        def put(name, shape, dt=F32, at=None, parts=P):
            size = 4 * int(np.prod(shape))
            if at is None:
                at = top[0]
                top[0] += (size + 31) // 32 * 32
            return nc.alloc_sbuf_tensor_at(name, [parts, *shape], dt, offset=at)

        def region(size):
            at = top[0]
            top[0] += (size + 31) // 32 * 32
            return at

        B = 4 * T
        wraw = [put(f"wraw{i}", [D]) for i in range(RAW)]
        whi = [put(f"whi{i}", [D], F32R) for i in range(RING)]
        wlo = [put(f"wlo{i}", [D], F32R) for i in range(RING)]
        hhi = [put(f"hhi{k}", [T], F32R) for k in range(KD)]
        hlo = [put(f"hlo{k}", [T], F32R) for k in range(KD)]
        yhi = [put(f"yhi{k}", [T], F32R) for k in range(KD)]
        ylo = [put(f"ylo{k}", [T], F32R) for k in range(KD)]
        r1 = region(16 * B)
        mhi = [put(f"mhi{k}", [T], F32R, r1 + k * B) for k in range(KD)]
        mlo = [put(f"mlo{k}", [T], F32R, r1 + (KD + k) * B) for k in range(KD)]
        r2 = region(KD * B)
        xin = put("xin", [KD, T], F32, r2)
        own = region(2 * B)
        hg = [r1 + i * B for i in range(16)] + [r2 + i * B for i in range(8)] + [own, own + B]
        names = ["b", "d", "dl", "e1", "e2", "e4", "e30", "e31", "q20", "q21", "ga0", "ga1", "ga2", "os",
                 "osq", "rst", "og0", "og1", "sf0", "sf1", "qf0", "qf1", "kin0", "kin1", "vt", "logf"]
        buf = {n: put("h_" + n, [T], F32, at) for n, at in zip(names, hg)}
        sf = [buf["sf0"], buf["sf1"]]
        qf = [buf["qf0"], buf["qf1"]]
        kin = [buf["kin0"], buf["kin1"]]
        ga = [buf["ga0"], buf["ga1"], buf["ga2"]]
        e3 = [buf["e30"], buf["e31"]]
        q2 = [buf["q20"], buf["q21"]]
        og = [buf["og0"], buf["og1"]]
        vt, logf, bc, dd, dl = buf["vt"], buf["logf"], buf["b"], buf["d"], buf["dl"]
        e1, e2, e4 = buf["e1"], buf["e2"], buf["e4"]
        o_sb, osq, rst = buf["os"], buf["osq"], buf["rst"]
        r3 = region(10 * B + 128)
        gA = [put(f"gA{i}", [T], F32, r3 + a * B) for i, a in enumerate((0, 2, 4))]
        gB = [put(f"gB{i}", [T], F32, r3 + a * B) for i, a in enumerate((1, 3, 5))]
        mA = [put(f"mA{i}", [T], F32, r3 + (6 + i) * B) for i in range(2)]
        mB = [put(f"mB{i}", [T], F32, r3 + (8 + i) * B) for i in range(2)]
        s_all = put("s_all", [4, P], F32, r3)
        h0 = [put(f"h0_{k}", [T], F32, r3 + k * B) for k in range(KD)]
        bg_own = region(B)
        bg = [put("bg0", [T], F32, bg_own), put("bg1", [T], F32, r3 + 4 * B), put("bg2", [T], F32, r3 + 5 * B)]
        pa = put("pa", [BUF + T], F32, r3 + 6 * B)
        pb = put("pb", [BUF + T], F32, r3 + 6 * B + 1728)
        pooled = [put(f"pooled{i}", [T], F32, r3 + 6 * B + 3456 + i * B) for i in range(2)]
        h32 = [put(f"h32_{i}", [T], F32, r3 + (4 + i) * B) for i in range(2)]
        ysq = [put(f"ysq{i}", [T], F32, r3 + i * B) for i in range(2)]
        yacc = put("yacc", [T], F32, r3 + 6 * B)
        yrs = put("yrs", [T], F32, r3 + 8 * B)
        xsq = [put(f"xsq{i}", [T]) for i in range(2)]
        xacc_at = region(B)
        xacc = put("xacc", [T], F32, xacc_at)
        sqh_at = region(B)
        sqh = put("sqh", [T], F32R, sqh_at)
        sql = {n: put(f"sql_{n}", [T], F32R, at) for n, at in (("head", hg[names.index("osq")]), ("x", xacc_at),
                                                               ("y", r3 + 6 * B))}
        xrs = xsq[0]
        xr_at = region(KD * B)
        xres = put("xres", [KD, T], F32, xr_at)
        s0 = [put(f"s0_{i}", [NB, P], F32, at) for i, at in enumerate((r3 + 4 * 4 * P, xr_at))]
        snew = [put(f"snew{i}", [NB, P], F32, at) for i, at in enumerate((r3 + 4 * B, xr_at + 4 * NB * P))]
        ktm = put("ktm", [4, P])
        vtm = put("vtm", [4, P])
        vms = [put(f"vms{i}", [4, P]) for i in range(2)]
        kj_at = top[0]
        kj2 = put("kj2", [NG, 2, CHUNK])
        q23 = put("q23", [NG, 2, CHUNK])
        kj4 = put("kj4", [NG, 4, CHUNK])
        q4 = [put(f"q4_{i}", [NG, 4, CHUNK]) for i in range(2)]
        wph, wplo = put("wph", [G, P], F32R, kj_at), put("wplo", [G, P], F32R, kj_at + 4 * G * P)
        assert kj_at + 8 * G * P <= top[0]
        pooled_hi = [put(f"pooled_hi{i}", [T], F32R, hg[names.index(n)]) for i, n in enumerate(("e1", "e2"))]
        pooled_lo = [put(f"pooled_lo{i}", [T], F32R, hg[names.index(n)]) for i, n in enumerate(("e4", "e30"))]
        dprev = put("dprev", [NG, 4])
        dfirst = put("dfirst", [NG, 4])
        dq = put("dq", [NG, 4])
        dg = put("dg", [NG])
        dh = put("dh", [NG])
        at_sb = put("at_sb", [T])
        ats = put("ats", [SAMPLE])
        carry = put("carry", [H, P])
        EXT = BUF + T
        ext = put("ext", [G, EXT])
        exts = put("exts", [G, NB, BUF + NT])
        pas = put("pas", [NB, BUF + NT])
        pbs = put("pbs", [NB, BUF + NT])
        wpl = put("wpl", [G, P])
        cst = put("cst", [C_N])
        smask = put("smask", [T])
        smask_s = put("smask_s", [SAMPLE])
        cmask = put("cmask", [NG, P])
        cmask_s = put("cmask_s", [NB, NT])
        bmask = put("bmask", [NB])
        ones = put("ones", [P], F32, sqh_at)
        ones_r = put("ones_r", [P], F32R)
        ident = put("ident", [P])
        lb = put("lb", [8, H])
        eps_t = put("eps_t", [1])
        rc = put("rc", [G, BUF])
        ptmp = put("ptmp", [BUF])
        assert top[0] <= nc.sbuf_usable_end, (top[0], nc.sbuf_usable_end)
        lb0, oml, noml = lb[:, 0], lb[:, 1], lb[:, 2]

        Z = [ctx.enter_context(nc.psum_tensor(f"Z{i}", [P, 512], F32)) for i in range(NZ)]
        B4, B5, B6, B7 = [ctx.enter_context(nc.psum_tensor(f"B{i}", [P, 512], F32)) for i in range(4, 8)]

        def sem(name):
            return ctx.enter_context(nc.semaphore(name))

        w_landed = [sem(f"w_landed{i}") for i in range(RAW)]
        x0_landed = [sem(f"x0_landed{i}") for i in range(4)]
        xin_landed, xres_landed, cst_landed = sem("xin_landed"), sem("xres_landed"), sem("cst_landed")
        wpl_landed = sem("wpl_landed")
        s0_landed, buf_landed = [sem(f"s0_landed{i}") for i in range(2)], sem("buf_landed")
        y_stored, snew_stored, ends_stored = sem("y_stored"), sem("snew_stored"), sem("ends_stored")
        acc_done, tv_done, tk_done, sc_done = sem("acc_done"), sem("tv_done"), sem("tk_done"), sem("sc_done")
        p_done, o_done, ssq_done, mix_done = sem("p_done"), sem("o_done"), sem("ssq_done"), sem("mix_done")
        xssq_done, yssq_done = sem("xssq_done"), sem("yssq_done")
        whi_made, sq_made, sg_made, sb_made = sem("whi_made"), sem("sq_made"), sem("sg_made"), sem("sb_made")
        logf_made, exp_made, osq_made, rst_made = sem("logf_made"), sem("exp_made"), sem("osq_made"), sem("rst_made")
        xsq_made, xrs_made, hhi_made = sem("xsq_made"), sem("xrs_made"), sem("hhi_made")
        yhi_made, mhi_made, ysq_made, yrs_made = sem("yhi_made"), sem("mhi_made"), sem("ysq_made"), sem("yrs_made")
        lbe_made = sem("lbe_made")
        wlo_made, kin_made, b_made, d_made = sem("wlo_made"), sem("kin_made"), sem("b_made"), sem("d_made")
        q_made, s_made, s0_copied, og_made = sem("q_made"), sem("s_made"), sem("s0_copied"), sem("og_made")
        t1_made, ylo_made, rc_used, pooled_made = sem("t1_made"), sem("ylo_made"), sem("rc_used"), sem("pooled_made")
        hist_kept, ybm_made, mlo_made = sem("hist_kept"), sem("ybm_made"), sem("mlo_made")
        h32_made, hlo_made, y_made, vms_made = sem("h32_made"), sem("hlo_made"), sem("y_made"), sem("vms_made")
        lb_made, zeroed, ptmp_made = sem("lb_made"), sem("zeroed"), sem("ptmp_made")
        wph_made, wplo_made, pmh_made, pml_made = sem("wph_made"), sem("wplo_made"), sem("pmh_made"), sem("pml_made")
        x0_summed, gained = sem("x0_summed"), sem("gained")
        kj_made, dq_made, ktm_made = sem("kj_made"), sem("dq_made"), sem("ktm_made")
        ssplit, xsplit, ysplit = sem("ssplit"), sem("xsplit"), sem("ysplit")
        ssplit_hi, xsplit_hi, ysplit_hi = sem("ssplit_hi"), sem("xsplit_hi"), sem("ysplit_hi")
        k_made, win_made, merged = sem("k_made"), sem("win_made"), sem("merged")
        xacc_made, yacc_made, masks = sem("xacc_made"), sem("yacc_made"), sem("masks")
        y_made_pool = sem("y_made_pool")
        z_read = [sem(f"z_read{i}") for i in range(NZ)]
        b4_read, b5_read = sem("b4_read"), sem("b5_read")

        def first(t):
            return isinstance(t, int) and t == 0

        def nth(t, per, i):
            return t * per + (i + 1)

        def acc_ready(t, kind, i):
            return nth(t, NA, ACC[(kind, i)])

        def z_bank(kind, i):
            return Z[ACC[(kind, i)] % NZ]

        def z_sem(kind, i):
            return z_read[ACC[(kind, i)] % NZ]

        def z_done(t, kind, i):
            return nth(t, NA // NZ, ACC[(kind, i)] // NZ)

        def b4_done(t, use, h):
            return nth(t, len(B4_USES), B4_USES.index((use, h))) + 1

        def b5_done(t, use, h):
            return nth(t, len(B5_USES), B5_USES.index((use, h)))

        def landed(t, n):
            return 16 * (t * (NU // RAW) + n // RAW + 1)

        def s_value(t, last, h, i):
            return t * 4 * H + h * (NG + NB if last else 4) + i + 1

        def p_value(t, last, h, i):
            return t * H + h * (3 if last else 1) + i + 1

        def win_value(t, last, g, level, sample=False):
            before = sum(range(1, g + 1)) * (2 if last else 1)
            return t * 10 + before + (2 * level + sample if last else level) + 1

        def pooled_value(t, last, g):
            return t * G + g + 1

        block = ctx.enter_context(nc.Block())

        @block.sync
        def _(sp):
            for i in range(4):
                sp.dma_start(xin[:, 2 * i:2 * i + 2, :], xT[0, :, 2 * i:2 * i + 2, :]).then_inc(x0_landed[i], 16)
                if i == 0:
                    sp.dma_start(cst[:], consts).then_inc(cst_landed, 16)
            for n in range(RAW):
                sp.dma_start(wraw[n][:], w_all[n]).then_inc(w_landed[n], 16)
            sp.dma_start(wpl[:], w_pool).then_inc(wpl_landed, 16)
            sp.dma_start(exts[:, :, :, 0:BUF], buf_in).then_inc(buf_landed, 16)

            def tile(t, last):
                for s in range(NU):
                    n = s + RAW
                    if n < NU or not last:
                        sp.wait_ge(wlo_made, nth(t, NU, s))
                        sp.dma_start(wraw[n % RAW][:], w_all[n % NU]).then_inc(w_landed[n % RAW], 16)
                    if s == 29 and not last:
                        sp.wait_ge(ylo_made, nth(t, 8, 7))
                        sp.dma_start(xin[:], xT[t + 1]).then_inc(xin_landed, 16)
                    if s == 11 and not first(t):
                        y_store(t - 1)
                    if s == 6 and last:
                        sp.wait_ge(ysplit, t)
                        sp.dma_start(s0[0][:], s_in[0]).then_inc(s0_landed[0], 16)
                    if s == 14 and last:
                        sp.wait_ge(y_stored, 16 * (TILES - 1))
                        sp.dma_start(s0[1][:], s_in[1]).then_inc(s0_landed[1], 16)
                    if last and s in (15, 19, 23, 27):
                        h = (s - 15) // 4
                        sp.wait_ge(s_made, s_value(t, last, h, NG + NB - 1))
                        sp.dma_start(ss_out[h], snew[min(h, 1)][:]).then_inc(snew_stored, 16)
                        if h < 2:
                            sp.wait_ge(o_done, nth(t, H, h))
                            sp.dma_start(s0[h][:], s_in[h + 2]).then_inc(s0_landed[h], 16)
                    if s == 32:
                        if last:
                            sp.wait_ge(snew_stored, 16 * H)
                        else:
                            sp.wait_ge(y_stored, t * 16)
                        sp.dma_start(xres[:], xT[t]).then_inc(xres_landed, 16)
                if last:
                    sp.dma_start(sp_out, carry[:]).then_inc(ends_stored, 16)
                    sp.wait_ge(ybm_made, nth(t, G, G - 1))
                    sp.dma_start(pp_out, ext[:, :, PT:PT + BUF]).then_inc(ends_stored, 16)
                    sp.dma_start(ps_out, exts[:, :, :, NT:NT + BUF]).then_inc(ends_stored, 16)
                    parts = [(POOL_OUT, POOL_OUT + 2), (0, 2), (POOL_OUT + 2, KD - 1), (KD - 1, KD), (2, POOL_OUT)]
                    for lo, hi in parts:
                        if hi <= POOL_OUT:
                            sp.wait_ge(y_made_pool, hi)
                        else:
                            sp.wait_ge(y_made, t * KD + hi - POOL_OUT)
                        sp.dma_start(yT[t, :, lo:hi, :], xres[:, lo:hi, :]).then_inc(y_stored, 16)
                    sp.wait_ge(ends_stored, 48)
                    sp.wait_ge(snew_stored, 16 * H)
                    sp.wait_ge(y_stored, 16 * (TILES - 1 + len(parts)))

            def y_store(t):
                sp.wait_ge(y_made, nth(t, KD, KD - 1))
                sp.dma_start(yT[t], xres[:]).then_inc(y_stored, 16)

            tile(0, False)
            with sp.Fori(1, TILES - 1) as t:
                tile(t, False)
            tile(TILES - 1, True)

        @block.tensor
        def _(pe):
            def three(out, parts, k_rhs, first, final):
                (wh, wl), (xh, xl) = parts, k_rhs
                pe.matmul(out, wh, xh, start=first, stop=False)
                pe.matmul(out, wh, xl, start=False, stop=False)
                return pe.matmul(out, wl, xh, start=False, stop=final)

            def small(t, last, s):
                for h in range(H):
                    base = 4 * h
                    if s == base + 12:
                        pe.wait_ge(ssplit, nth(t, H, h))
                        pe.wait_ge(b4_read, b4_done(t, "ssq", h) - 1)
                        sum_squares(B4, "head").then_inc(ssq_done, 1)
                    if s == base + 6:
                        pe.wait_ge(z_sem("i", h), z_done(t, "i", h))
                        pe.wait_ge(b5_read, b5_done(t, "tv", h) - 1)
                        transposes(B5, vt, tv_done, vt)
                    if s == base + 7:
                        pe.wait_ge(kj_made, nth(t, KJ * H, KJ * h + KJ - 1))
                        if not h:
                            pe.wait_ge(ybm_made, t * G)
                        elif last:
                            pe.wait_ge(s_made, s_value(t, last, h - 1, NG + 3))
                        else:
                            pe.wait_ge(ktm_made, nth(t, H, h - 1))
                        transposes(B7, kj4[:].rearrange("p g j n -> p (g j n)"), tk_done, e4)
                        pe.wait_ge(q_made, nth(t, 3 * H, 3 * h + 1))
                        pe.wait_ge(k_made, nth(t, 2 * H, 2 * h + 1))
                        pe.wait_ge(b4_read, b4_done(t, "scores", h) - 1)
                        for g in range(NG):
                            c = slice(g * P, (g + 1) * P)
                            pe.matmul(B4[:, c], e2[:, c], e1[:, c], start=True, stop=True)
                            for j in (0, 2):
                                at = g * P + j * CHUNK
                                c = slice(at + CHUNK, at + 2 * CHUNK)
                                pe.matmul(B4[j * CHUNK:(j + 1) * CHUNK, c], e4[:, at:at + CHUNK], q2[h % 2][:, c],
                                          start=True, stop=True)
                            c = slice(g * P + 2 * CHUNK, (g + 1) * P)
                            pe.matmul(B4[0:2 * CHUNK, c], kj2[:, g].rearrange("p j n -> p (j n)"),
                                      q23[:, g].rearrange("p j n -> p (j n)"), start=True, stop=True)
                        pe.matmul(B4[0:SAMPLE, PT:T], e2[:, PT:T], e1[:, PT:T], start=True,
                                  stop=True).then_inc(sc_done, 1)
                    if s == base + 8:
                        pe.wait_ge(ktm_made, nth(t, H, h))
                        pe.wait_ge(b5_read, b5_done(t, "tv", h))
                        if h:
                            pe.wait_ge(s_made, s_value(t, last, h - 1, NG + NB - 1 if last else 3))
                        else:
                            pe.wait_ge(ybm_made, t * G)
                        for g in range(NG):
                            mm = pe.matmul(B6[:, g * P:(g + 1) * P], ktm[:, g, :], vtm[:, g, :], start=True, stop=True)
                        if not last:
                            mm = pe.matmul(B6[:, 3 * P:4 * P], ktm[0:CHUNK, 3, :], vtm[0:CHUNK, 3, :], start=True,
                                           stop=True)
                        mm.then_inc(p_done, 1)
                        if last:
                            pe.wait_ge(vms_made, 2 * h + 1)
                            sample_products(B7, vms[0])
                    if s == base + 9:
                        outputs(t, last, h)
                    if s == base + 9 and last:
                        pe.wait_ge(s_made, s_value(t, last, h, NG - 1))
                        pe.wait_ge(vms_made, 2 * h + 2)
                        sample_products(B6, vms[1])
                if s in MIX_SLOT:
                    g = MIX_SLOT[s]
                    pe.wait_ge(wplo_made, t + 1)
                    pe.wait_ge(pml_made, nth(t, G, g))
                    if g == 1:
                        pe.wait_ge(ktm_made, nth(t, H, H - 1))
                    if g < 2:
                        pe.wait_ge(s_made, s_value(t, last, H - 1, NG + NB - 1 if last else 3))
                    else:
                        pe.wait_ge(ybm_made, nth(t, G, g - 2))
                    three((B6, B7)[g % 2][:, 0:T], (wph[:, g, :], wplo[:, g, :]),
                          (pooled_hi[g % 2][:], pooled_lo[g % 2][:]), True, True).then_inc(mix_done, 1)
                if s == XNORM and not last:
                    pe.wait_ge(b4_read, b4_done(t, "xssq", 0) - 1)
                    pe.wait_ge(xsplit, t + 1)
                    sum_squares(B4, "x").then_inc(xssq_done, 1)
                if s == YNORM and not first(t):
                    y_squares(t - 1, False)

            def transposes(bank, src, done, rest):
                for g in range(NG):
                    pe.transpose(bank[:, g * P:(g + 1) * P], src[:, g * P:(g + 1) * P], ident[:])
                pe.transpose(bank[0:SAMPLE, 3 * P:4 * P], rest[:, PT:T], ident[:]).then_inc(done, 1)

            def sample_products(bank, v):
                pe.matmul(bank[:], ktm[0:SAMPLE, 3, :], v[0:SAMPLE], start=True, stop=True).then_inc(p_done, 1)

            def y_squares(t, last):
                pe.wait_ge(ysplit, t + 1)
                pe.wait_ge(b5_read, b5_done(t, "yssq", 0) - 1)
                mm = sum_squares(B5, "y", not last)
                if last:
                    pe.wait_ge(ysq_made, nth(t, KD, KD - 1))
                    mm = pe.matmul(B5[:, 0:T], ones_r[:].bitcast(F32), ysq[(KD - 1) % 2][:], start=False, stop=True)
                mm.then_inc(yssq_done, 1)

            def sum_squares(bank, what, final=True):
                pe.matmul(bank[:, 0:T], ones_r[:], sqh[:], start=True, stop=False)
                return pe.matmul(bank[:, 0:T], ones_r[:], sql[what][:], start=False, stop=final)

            def outputs(t, last, h):
                pe.wait_ge(b4_read, b4_done(t, "scores", h))
                pe.wait_ge(b5_read, b5_done(t, "o", h) - 1)
                for g in range(3):
                    c = slice(g * P, (g + 1) * P)
                    pe.matmul(B5[:, c], vtm[:, g, :], at_sb[:, c], start=(g == 0), stop=False,
                              skip_group_check=True)
                a3 = ats[0:SAMPLE, :] if last else at_sb[0:SAMPLE, PT:T]
                pe.matmul(B5[:, PT:T], vtm[0:SAMPLE, 3, :], a3, start=False, stop=False,
                          skip_group_check=True)
                pe.wait_ge(s_made, s_value(t, last, h, NG - 1))
                pe.wait_ge(s0_copied, nth(t, H, h))
                pe.wait_ge(q_made, nth(t, 3 * H, 3 * h + 2))
                for g in range(NG):
                    pe.matmul(B5[:, g * P:(g + 1) * P], s_all[:, g, :],
                              q4[h % 2][:, g].rearrange("p j n -> p (j n)"), start=False, stop=False,
                              skip_group_check=True)
                if not last:
                    mm = pe.matmul(B5[:, PT:T], s_all[:, 3, :], q2[h % 2][:, PT:T], start=False, stop=True,
                                   skip_group_check=True)
                if last:
                    pe.wait_ge(s0_landed[h % 2], 16 * (h // 2 + 1))
                    for b in range(NB):
                        c = PT + b * NT
                        mm = pe.matmul(B5[:, c:c + NT], s0[h % 2][:, b, :], q2[h % 2][:, c:c + NT],
                                       start=False, stop=(b == NB - 1), skip_group_check=True)
                mm.then_inc(o_done, 1)

            def product(t, s, acc, blocks):
                opened(t, acc)
                out = Z[ACC[acc] % NZ][:, 0:T]
                for i, (k, hi, lo, ready, value) in enumerate(blocks):
                    if ready is not None:
                        pe.wait_ge(ready, value)
                    mm = part(s, out, k, hi, lo, i == 0, i == len(blocks) - 1)
                mm.then_inc(acc_done, 1)

            def opened(t, acc):
                n = ACC[acc]
                pe.wait_ge(z_read[n % NZ], t * (NA // NZ) + n // NZ)

            def part(s, out, k, hi, lo, first, final):
                c = slice(k * P, (k + 1) * P)
                return three(out, (whi[s % RING][:, c], wlo[s % RING][:, c]), (hi[:], lo[:]), first, final)

            def tile(t, last):
                for s, (kind, i) in enumerate(UNITS):
                    small(t, last, s)
                    if first(t) and s < 2:
                        if s == 0:
                            first_units()
                        continue
                    pe.wait_ge(wlo_made, nth(t, NU, s))
                    if kind == "y":
                        def ready(k):
                            return (ylo_made, nth(t, 8, Y_ORDER.index(k))) if i == 0 else (None, None)
                        product(t, s, ("ya", i), [(k, yhi[k], ylo[k], *ready(k)) for k in range(4)])
                        product(t, s, ("yb", i), [(k, yhi[k], ylo[k], *ready(k)) for k in range(4, 8)])
                    elif kind == "out" and i < 2:
                        if i == 0:
                            pe.wait_ge(wlo_made, nth(t, NU, s + 1))
                            for u in range(2):
                                opened(t, ("out", u))
                                for k in range(KD - 1):
                                    if u == 0:
                                        pe.wait_ge(mlo_made, nth(t, KD, k))
                                    part(s + u, Z[ACC[("out", u)] % NZ][:, 0:T], k, mhi[k], mlo[k], k == 0, False)
                            pe.wait_ge(mlo_made, nth(t, KD, KD - 1))
                            for u in range(2):
                                part(s + u, Z[ACC[("out", u)] % NZ][:, 0:T], KD - 1, mhi[KD - 1], mlo[KD - 1], False,
                                     True).then_inc(acc_done, 1)
                    elif kind == "out":
                        product(t, s, (kind, i), [(k, mhi[k], mlo[k], None, None) for k in range(KD)])
                    else:
                        product(t, s, (kind, i), [
                            (k, hhi[k], hlo[k], *((hlo_made, nth(t, KD, k)) if s == 0 else (None, None)))
                            for k in range(KD)])
                if last:
                    y_squares(t, True)

            def first_units():
                for u in range(2):
                    pe.wait_ge(wlo_made, u + 1)
                    for k in range(KD):
                        if u == 0:
                            pe.wait_ge(hhi_made, k + 1)
                        c = slice(k * P, (k + 1) * P)
                        pe.matmul(Z[u][:, 0:T], whi[u][:, c], hhi[k][:], start=(k == 0), stop=False)
                        pe.matmul(Z[u][:, 0:T], wlo[u][:, c], hhi[k][:], start=False, stop=False)
                for k in range(KD):
                    pe.wait_ge(hlo_made, k + 1)
                    for u in range(2):
                        mm = pe.matmul(Z[u][:, 0:T], whi[u][:, k * P:(k + 1) * P], hlo[k][:], start=False,
                                       stop=(k == KD - 1))
                        if k == KD - 1:
                            mm.then_inc(acc_done, 1)

            pe.wait_ge(zeroed, ZEROED)
            for i in range(2):
                pe.wait_ge(x0_summed, KD - 3 + i)
                mm = pe.matmul(B4[:, 0:T], ones_r[:].bitcast(F32), h0[i][:], start=(i == 0), stop=(i == 1))
            mm.then_inc(xssq_done, 1)
            pe.wait_ge(masks, MASKS)
            tile(0, False)
            with pe.Fori(1, TILES - 1) as t:
                tile(t, False)
            tile(TILES - 1, True)

        @block.scalar
        def _(act):
            def split(t, n):
                act.wait_ge(w_landed[n % RAW], landed(t, n))
                act.activation(whi[n % RING][:], wraw[n % RAW][:], ACT.Copy).then_inc(whi_made, 1)

            def x_square(t, k):
                if k == 0:
                    act.wait_ge(xin_landed, 16 * t + 16)
                if k >= 3:
                    act.wait_ge(xacc_made, nth(t, KD - 1, k - 3))
                act.activation(xacc[:] if k == 0 else xsq[k % 2][:], xin[:, k, :],
                               ACT.Square).then_inc(xsq_made, 1)

            def x_norm(value):
                act.wait_ge(xssq_done, value)
                act.activation(xrs[:], B4[:, 0:T], ACT.Ln, bias=eps_t[:], scale=1.0 / D).then_inc(b4_read, 1)

            def x_norm_exp(value, b4_value):
                act.wait_ge(b4_read, b4_value)
                act.activation(xrs[:], xrs[:], ACT.Exp, scale=-0.5).then_inc(xrs_made, 1)

            def h_hi(value, k, src=None):
                act.wait_ge(h32_made, (value - 1) * KD + k + 1)
                act.activation(hhi[k][:], (src or h32[k % 2])[:], ACT.Copy).then_inc(hhi_made, 1)

            def sigmoid(t, kind, i, out, done):
                act.wait_ge(acc_done, acc_ready(t, kind, i))
                act.activation(out[:], z_bank(kind, i)[:, 0:T], ACT.Sigmoid).then_inc(done, 1)

            def decays(t, last, h):
                act.wait_ge(z_sem("f", h), z_done(t, "f", h))
                act.activation(logf[:], sf[h % 2][:], ACT.Ln, bias=lb0[:, h:h + 1],
                               scale=oml[:, h:h + 1]).then_inc(logf_made, 1)
                act.wait_ge(b_made, nth(t, H, h))
                act.activation(e3[h % 2][:], bc[:], ACT.Exp).then_inc(exp_made, 1)
                act.wait_ge(d_made, nth(t, 2 * H, 2 * h))
                act.activation(e1[:], dd[:], ACT.Exp).then_inc(exp_made, 1)
                act.activation(e2[:], dd[:], ACT.Exp, scale=-1.0).then_inc(exp_made, 1)
                act.wait_ge(d_made, nth(t, 2 * H, 2 * h + 1))
                act.activation(e4[:], dl[:], ACT.Exp).then_inc(exp_made, 1)

            def head_norm(t, h):
                act.wait_ge(ssq_done, nth(t, H, h))
                act.activation(rst[:], B4[:, 0:T], ACT.Ln, bias=eps_t[:], scale=1.0 / P).then_inc(b4_read, 1)
                act.wait_ge(b4_read, b4_done(t, "ssq", h))
                act.activation(rst[:], rst[:], ACT.Exp, scale=-0.5).then_inc(rst_made, 1)

            def tile(t, last):
                for s in range(NU):
                    if s + AHEAD < NU or not last:
                        act.wait_ge(acc_done, t * NA + (LAST_ACC[s - 1] + 1 if s else 0))
                        split(t, s + AHEAD)
                    if s == 0 and not first(t):
                        y_square(t - 1, KD - 1)
                    for h in range(H):
                        if s == 4 * h + 1:
                            sigmoid(t, "f", h, sf[h % 2], z_sem("f", h))
                        if s == 4 * h + 2:
                            sigmoid(t, "q", h, qf[h % 2], sq_made)
                        if s == 4 * h + 3:
                            act.wait_ge(acc_done, acc_ready(t, "i", h))
                            act.activation(vt[:], z_bank("i", h)[:, 0:T], ACT.Copy).then_inc(z_sem("i", h), 1)
                        if s == 4 * h + 4:
                            sigmoid(t, "g", h, ga[h % 3], sg_made)
                        if s == 4 * h + 6:
                            act.wait_ge(tv_done, nth(t, H, h))
                            act.activation(vtm[:, 0:3, :], B5[:, 0:3 * P].rearrange("p (g v) -> p g v", v=P), ACT.Copy)
                            act.activation(vtm[0:SAMPLE, 3, :], B5[0:SAMPLE, 3 * P:4 * P],
                                           ACT.Copy).then_inc(b5_read, 1)
                        if s == 4 * h + 9:
                            act.wait_ge(o_done, nth(t, H, h))
                            act.activation(osq[:], B5[:, 0:T], ACT.Square).then_inc(osq_made, 1)
                            act.activation(o_sb[:], B5[:, 0:T], ACT.Copy).then_inc(b5_read, 1)
                        if s == 4 * h + 13:
                            act.wait_ge(og_made, nth(t, H, h))
                            act.activation(yhi[h][:], og[h % 2][:], ACT.Copy).then_inc(yhi_made, 1)
                    if s % 4 == 0 and 4 <= s <= 24:
                        act.preload_act_table_set(LN_EXP)
                        if s <= 16:
                            decays(t, last, s // 4 - 1)
                        if s >= 12:
                            head_norm(t, s // 4 - 3)
                        if s == 4 and not first(t):
                            y_norm(t - 1)
                    for g in range(G):
                        if s == 17 + 2 * g:
                            act.wait_ge(acc_done, acc_ready(t, "u", g))
                            act.wait_ge(hist_kept, t * G)
                            z = z_bank("u", g)
                            if last:
                                act.activation(ext[:, g, BUF:BUF + PT], z[:, 0:PT], ACT.Copy)
                                act.activation(exts[:, g, :, BUF:BUF + NT],
                                               z[:, PT:T].rearrange("p (b n) -> p b n", n=NT),
                                               ACT.Copy).then_inc(z_sem("u", g), 1)
                            else:
                                act.activation(ext[:, g, BUF:EXT], z[:, 0:T], ACT.Copy).then_inc(z_sem("u", g), 1)
                        if s == 18 + 2 * g:
                            if g == 3:
                                act.wait_ge(ylo_made, nth(t, 8, Y_ORDER.index(4)))
                            sigmoid(t, "b", g, bg[g % 3], sb_made)
                    if s == 20:
                        if first(t):
                            act.wait_ge(wpl_landed, 16)
                        act.wait_ge(sc_done, nth(t, H, H - 1))
                        act.activation(wph[:], wpl[:], ACT.Copy).then_inc(wph_made, 1)
                    if s in MEANS_SPLIT:
                        g = MEANS_SPLIT[s]
                        act.wait_ge(pooled_made, pooled_value(t, last, g))
                        if g == 0:
                            act.wait_ge(sc_done, nth(t, H, H - 1))
                        if g >= 2:
                            act.wait_ge(mix_done, nth(t, G, g - 2))
                        act.activation(pooled_hi[g % 2][:], pooled[g % 2][:], ACT.Copy).then_inc(pmh_made, 1)
                    if s in MIX_SLOT:
                        g = MIX_SLOT[s]
                        act.wait_ge(ybm_made, nth(t, G, g))
                        act.activation(yhi[4 + g][:], bg[g % 3][:], ACT.Copy).then_inc(yhi_made, 1)
                    kind, j = UNITS[s - 1] if s else (None, 0)
                    if kind == "ma":
                        sigmoid(t, "ma", j, gA[j % 3], z_sem("ma", j))
                    if kind == "mb":
                        sigmoid(t, "mb", j, gB[j % 3], z_sem("mb", j))
                    if s in XSQ_SLOT and not last:
                        x_square(t, XSQ_SLOT[s])
                    if s == XNORM and not last:
                        act.preload_act_table_set(LN_EXP)
                        x_norm(t + 2)
                        x_norm_exp(t + 2, b4_done(t, "xssq", 0))
                    if kind == "y":
                        act.wait_ge(merged, nth(t, KD, j))
                        act.activation(mhi[j][:], mA[j % 2][:], ACT.Copy).then_inc(mhi_made, 1)
                    if s in H_SLOT and not last:
                        h_hi(t + 2, H_SLOT[s])
                    if kind == "out":
                        y_square(t, j)
                if last:
                    y_square(t, KD - 1)
                    act.preload_act_table_set(LN_EXP)
                    y_norm(t)

            def y_norm(t):
                act.wait_ge(yssq_done, t + 1)
                act.activation(yrs[:], B5[:, 0:T], ACT.Ln, bias=eps_t[:], scale=1.0 / D).then_inc(b5_read, 1)
                act.wait_ge(b5_read, b5_done(t, "yssq", 0))
                act.activation(yrs[:], yrs[:], ACT.Exp, scale=-0.5).then_inc(yrs_made, 1)

            def y_square(t, j):
                act.wait_ge(z_sem("out", j), z_done(t, "out", j))
                if j >= 3:
                    act.wait_ge(yacc_made, nth(t, KD - 1, j - 3))
                act.activation(yacc[:] if j == 0 else ysq[j % 2][:], xres[:, j, :], ACT.Square).then_inc(ysq_made, 1)

            act.preload_act_table_set(LN_EXP)
            act.wait_ge(zeroed, ZEROED)
            for k in range(KD):
                act.wait_ge(x0_landed[k // 2], 16)
                act.activation(h0[k][:], xin[:, k, :], ACT.Square).then_inc(xsq_made, 1)
                if k == 3:
                    act.wait_ge(lb_made, 3)
                    act.activation(lb[:, 3:5], lb[:, 3:5], ACT.Exp).then_inc(lbe_made, 1)
            split(0, 0)
            x_norm(1)
            x_norm_exp(1, 1)
            for k in range(KD):
                if k == 2:
                    split(0, 1)
                h_hi(1, k, h0[k])
            for n in range(2, AHEAD):
                split(0, n)
            act.wait_ge(lb_made, LB_STEPS)
            tile(0, False)
            with act.Fori(1, TILES - 1) as t:
                tile(t, False)
            tile(TILES - 1, True)

        @block.vector
        def _(dve):
            def split(t, n):
                dve.wait_ge(whi_made, nth(t, NU, n))
                dve.tensor_tensor(wlo[n % RING][:], wraw[n % RAW][:], whi[n % RING][:].bitcast(F32),
                                  ALU.subtract).then_inc(wlo_made, 1)

            def h_block(value, k):
                if k == 0:
                    dve.wait_ge(xrs_made, value)
                if 2 <= k < KD:
                    dve.wait_ge(hlo_made, (value - 1) * KD + k - 1)
                if k < KD:
                    dve.scalar_tensor_tensor(out=h32[k % 2][:], in0=xin[:, k, :],
                                             scalar=cst[:, C_NG + k:C_NG + k + 1], in1=xrs[:], op0=ALU.mult,
                                             op1=ALU.mult).then_inc(h32_made, 1)
                if k:
                    dve.wait_ge(hhi_made, (value - 1) * KD + k)
                    dve.tensor_tensor(hlo[k - 1][:], h32[(k - 1) % 2][:], hhi[k - 1][:].bitcast(F32),
                                      ALU.subtract).then_inc(hlo_made, 1)

            def gated(t, kind, i, out, made, scalar):
                dve.wait_ge(made, nth(t, 4, i))
                dve.scalar_tensor_tensor(out=out[:], in0=z_bank(kind, i)[:, 0:T], scalar=scalar, in1=out[:],
                                         op0=ALU.mult, op1=ALU.mult).then_inc(z_sem(kind, i), 1)

            def sums(t, last, h):
                dve.wait_ge(logf_made, nth(t, H, h))
                parts = [(0, PT, CHUNK, smask[:, 0:PT]), (PT, T, NT, smask_s[:])] if last else [(0, T, CHUNK, smask[:])]
                for lo, hi, n, mask in parts:
                    ins = dve.tensor_tensor_scan(bc[:, lo:hi], mask, logf[:, lo:hi], 0.0, ALU.mult, ALU.add)
                ins.then_inc(b_made, 1)
                dve.wait_ge(b_made, nth(t, H, h))
                for out, at, sign in ((dd, 0, 1), (dl, 1, -1)):
                    for lo, hi, n, _ in parts:
                        v = bc[:, lo:hi].rearrange("p (c n) -> p c n", n=n)
                        m = n // 2 if at == 0 else n - 1
                        r = v[:, :, m:m + 1].broadcast_to([P, (hi - lo) // n, n])
                        o = out[:, lo:hi].rearrange("p (c n) -> p c n", n=n)
                        a, b = (v, r) if sign == 1 else (r, v)
                        ins = dve.tensor_tensor(o, a, b, ALU.subtract)
                    ins.then_inc(d_made, 1)

            def queries(t, h):
                dve.wait_ge(z_sem("q", h), z_done(t, "q", h))
                dve.wait_ge(exp_made, nth(t, 4 * H, 4 * h))
                dve.tensor_tensor(q2[h % 2][:], qf[h % 2][:], e3[h % 2][:], ALU.mult).then_inc(q_made, 1)
                dve.wait_ge(exp_made, nth(t, 4 * H, 4 * h + 1))
                dve.tensor_tensor(e1[:], qf[h % 2][:], e1[:], ALU.mult).then_inc(q_made, 1)
                dve.tensor_copy(dprev[:, :, 1:4], chunk_decay(h)[:, :, 0:3]).then_inc(dq_made, 1)
                dve.wait_ge(dq_made, nth(t, 3 * H, 3 * h))
                dve.tensor_tensor_scan(dq[:].rearrange("p g j -> p (g j)"), dprev[:].rearrange("p g j -> p (g j)"),
                                       dfirst[:].rearrange("p g j -> p (g j)"), 0.0, ALU.mult,
                                       ALU.add).then_inc(dq_made, 1)
                dve.wait_ge(dq_made, nth(t, 3 * H, 3 * h + 1))
                dve.tensor_tensor(dg[:], dq[:, :, 3], chunk_decay(h)[:, :, 3], ALU.mult).then_inc(dq_made, 1)
                dve.wait_ge(q_made, nth(t, 3 * H, 3 * h))
                dve.tensor_tensor(q4[h % 2][:].rearrange("p g j n -> p (g j) n"),
                                  q2[h % 2][:, 0:PT].rearrange("p (c n) -> p c n", n=CHUNK),
                                  dq[:].rearrange("p g j -> p (g j)").unsqueeze(2).broadcast_to([P, 4 * NG, CHUNK]),
                                  ALU.mult).then_inc(q_made, 1)

            def chunk_decay(h):
                return e3[h % 2][:, 0:PT].rearrange("p (g j n) -> p g j n", g=NG, n=CHUNK)[:, :, :, CHUNK - 1]

            def scores(t, last, h):
                dve.wait_ge(sc_done, nth(t, H, h))
                dve.wait_ge(o_done, t * H + h)
                if h == 0:
                    dve.wait_ge(s_made, t * H * 4)
                dve.tensor_copy(s_all[:, 0, :], carry[:, h, :]).then_inc(s0_copied, 1)
                dve.copy_predicated(at_sb[:, 0:PT], cmask[:].bitcast(U32).rearrange("p a b -> p (a b)"),
                                    B4[:, 0:PT])
                out3, mask3 = (ats[0:SAMPLE, :], cmask_s[0:SAMPLE]) if last else (
                    at_sb[0:SAMPLE, PT:T], cmask[0:SAMPLE, 0:1, 0:SAMPLE])
                dve.copy_predicated(out3, mask3.bitcast(U32).rearrange("p a b -> p (a b)"),
                                    B4[0:SAMPLE, PT:T]).then_inc(b4_read, 1)

            def decayed_keys(t, h):
                dve.wait_ge(k_made, nth(t, 2 * H, 2 * h + 1))
                k2 = e4[:, 0:PT].rearrange("p (g j n) -> p g j n", g=NG, n=CHUNK)
                q = q2[h % 2][:, 0:PT].rearrange("p (g j n) -> p g j n", g=NG, n=CHUNK)
                d = chunk_decay(h)

                def decayed(out, src, decay, n):
                    dve.tensor_tensor(out, src, decay.broadcast_to([P, NG, n * CHUNK]), ALU.mult).then_inc(kj_made, 1)

                dve.tensor_tensor(dh[:], d[:, :, 2], d[:, :, 3], ALU.mult).then_inc(kj_made, 1)
                decayed(kj2[:, :, 0, :], k2[:, :, 0, :], d[:, :, 1:2], 1)
                dve.tensor_copy(kj2[:, :, 1, :], k2[:, :, 1, :]).then_inc(kj_made, 1)
                decayed(q23[:, :, 1, :], q[:, :, 3, :], d[:, :, 2:3], 1)
                dve.tensor_copy(q23[:, :, 0, :], q[:, :, 2, :]).then_inc(kj_made, 1)
                decayed(kj4[:, :, 2, :], k2[:, :, 2, :], d[:, :, 3:4], 1)
                dve.tensor_copy(kj4[:, :, 3, :], k2[:, :, 3, :]).then_inc(kj_made, 1)
                dve.wait_ge(kj_made, nth(t, KJ * H, KJ * h + 2))
                decayed(kj4[:, :, 0:2, :].rearrange("p g j n -> p g (j n)"), kj2[:].rearrange("p g j n -> p g (j n)"),
                        dh[:].unsqueeze(2), 2)

            def update(t, last, h, g):
                if g == 0:
                    dve.wait_ge(p_done, p_value(t, last, h, 0))
                else:
                    dve.wait_ge(s_made, s_value(t, last, h, g - 1))
                s_in = s_all[:, g, :] if g else carry[:, h, :]
                s_out = carry[:, h, :] if g == (NG - 1 if last else NG) else s_all[:, g + 1, :]
                decay = dg[:, g:g + 1] if g < NG else e3[h % 2][:, T - 1:T]
                dve.scalar_tensor_tensor(out=s_out, in0=s_in, scalar=decay, in1=B6[:, g * P:(g + 1) * P],
                                         op0=ALU.mult, op1=ALU.add).then_inc(s_made, 1)

            def updates(t, last, h):
                for g in range(NG if last else NG + 1):
                    update(t, last, h, g)
                if last:
                    for b in range(4):
                        sample_update(t, h, b)

            def sample_update(t, h, b):
                if b % 4 == 0:
                    dve.wait_ge(p_done, p_value(t, True, h, 1 + b // 4))
                if b == 0:
                    dve.wait_ge(s0_landed[h % 2], 16 * (h // 2 + 1))
                    if h:
                        dve.wait_ge(snew_stored, 16 * h)
                e = PT + b * NT + NT - 1
                dve.scalar_tensor_tensor(out=snew[min(h, 1)][:, b, :], in0=s0[h % 2][:, b, :], scalar=e3[h % 2][:, e:e + 1],
                                         in1=(B7, B6)[b // 4][:, (b % 4) * P:(b % 4 + 1) * P], op0=ALU.mult,
                                         op1=ALU.add).then_inc(s_made, 1)

            def means(t, last, g):
                w = WINDOWS[g]
                src, srcs = (pb, pbs) if g % 2 else (pa, pas)
                n = PT if last else T
                dve.wait_ge(win_made, win_value(t, last, g, g, last))
                if g == 0:
                    dve.wait_ge(rc_used, RC_FIRST + t)
                if g >= 2:
                    dve.wait_ge(mix_done, nth(t, G, g - 2))
                dve.tensor_tensor(ptmp[:], src[:, BUF:2 * BUF], rc[:, g, :], ALU.mult).then_inc(ptmp_made, 1)
                dve.scalar_tensor_tensor(out=pooled[g % 2][:, BUF:n], in0=src[:, 2 * BUF:BUF + n], scalar=1.0 / w,
                                         in1=ext[:, g, 2 * BUF:BUF + n], op0=ALU.mult, op1=ALU.subtract)
                if last:
                    dve.scalar_tensor_tensor(
                        out=pooled[g % 2][:, PT:T].rearrange("p (b n) -> p b n", n=NT), in0=srcs[:, :, BUF:BUF + NT],
                        scalar=1.0 / w, in1=exts[:, g, :, BUF:BUF + NT], op0=ALU.mult, op1=ALU.subtract)
                dve.wait_ge(ptmp_made, nth(t, G, g))
                dve.tensor_tensor(pooled[g % 2][:, 0:BUF], ptmp[:], ext[:, g, BUF:2 * BUF],
                                  ALU.subtract).then_inc(pooled_made, 1)
                if not last:
                    dve.wait_ge(pooled_made, nth(t, G, g))
                    dve.tensor_copy(ext[:, g, 0:BUF], ext[:, g, T:T + BUF]).then_inc(hist_kept, 1)

            def merge(t, j):
                for acc, gate, out, n in (("ya", gA, mA, 0), ("yb", gB, mB, 1)):
                    dve.wait_ge(acc_done, acc_ready(t, acc, j))
                    dve.wait_ge(z_sem("m" + acc[1], j), z_done(t, "m" + acc[1], j))
                    dve.tensor_tensor(out[j % 2][:], z_bank(acc, j)[:, 0:T], gate[j % 3][:],
                                      ALU.mult).then_inc(z_sem(acc, j), 1)

            def merged_rest(t, j):
                dve.wait_ge(mhi_made, nth(t, KD, j))
                dve.tensor_tensor(mlo[j][:], mA[j % 2][:], mhi[j][:].bitcast(F32), ALU.subtract).then_inc(mlo_made, 1)

            def residual(t, j):
                if j == 0:
                    dve.wait_ge(xres_landed, 16 * t + 16)
                dve.wait_ge(acc_done, acc_ready(t, "out", j))
                dve.tensor_tensor(xres[:, j, :], z_bank("out", j)[:, 0:T], xres[:, j, :],
                                  ALU.add).then_inc(z_sem("out", j), 1)

            def tile(t, last):
                for s in range(NU):
                    kind, j = UNITS[s - 1] if s else (None, 0)
                    if kind == "y":
                        merge(t, j)
                    if s + AHEAD < NU or not last:
                        split(t, s + AHEAD)
                    if s == 0 and not first(t):
                        residual(t - 1, KD - 1)
                    if s == YNORM - 2 and not first(t):
                        y_split(t - 1, False)
                    if 5 <= s <= 8 and not first(t):
                        output(t - 1, range(2 * s - 10, 2 * s - 8))
                    if s % 4 == 2 and 10 <= s <= 22:
                        h = (s - 10) // 4
                        dve.wait_ge(osq_made, nth(t, H, h))
                        if h:
                            dve.wait_ge(ssq_done, nth(t, H, h - 1))
                        elif not first(t):
                            dve.wait_ge(yssq_done, t)
                        split_squares(osq, "head", (ssplit_hi, ssplit), nth(t, H, h))
                    if s == XNORM - 2 and not last:
                        dve.wait_ge(xacc_made, nth(t, KD - 1, KD - 2))
                        dve.wait_ge(ssq_done, nth(t, H, H - 1))
                        split_squares(xacc, "x", (xsplit_hi, xsplit), t + 1)
                    for h in range(H):
                        if s == 4 * h + 1:
                            dve.wait_ge(z_sem("f", h), z_done(t, "f", h))
                            dve.tensor_scalar(kin[h % 2][:], sf[h % 2][:], noml[:, h:h + 1], oml[:, h:h + 1],
                                              ALU.mult, ALU.add).then_inc(kin_made, 1)
                        if s == 4 * h + 2:
                            gated(t, "q", h, qf[h % 2], sq_made, QSCALE)
                        if s == 4 * h + 4:
                            gated(t, "g", h, ga[h % 3], sg_made, cst[:, C_GN:C_GN + 1])
                            if h and not last:
                                updates(t, last, h - 1)
                            sums(t, last, h)
                            if h and last:
                                updates(t, last, h - 1)
                            queries(t, h)
                        if s == 4 * h + 5:
                            decayed_keys(t, h)
                        if s == 4 * h + 7:
                            scores(t, last, h)
                            dve.wait_ge(tk_done, nth(t, H, h))
                            dve.tensor_copy(ktm[:, 0:3, :], B7[:, 0:3 * P].rearrange("p (g v) -> p g v", v=P))
                            dve.tensor_copy(ktm[0:SAMPLE, 3, :], B7[0:SAMPLE, 3 * P:4 * P]).then_inc(ktm_made, 1)
                        if s == 4 * h + 6:
                            if last:
                                dve.wait_ge(b5_read, b5_done(t, "tv", h))
                                for half in range(2):
                                    dve.tensor_tensor(
                                        vms[half][0:SAMPLE], vtm[0:SAMPLE, 3:4, :].broadcast_to([SAMPLE, 4, P]),
                                        bmask[0:SAMPLE, 4 * half:4 * half + 4].unsqueeze(2).broadcast_to([SAMPLE, 4, P]),
                                        ALU.mult).then_inc(vms_made, 1)
                        if s == 4 * h + 8 and h == H - 1:
                            updates(t, last, h)
                        if s == 4 * h + 9 and last:
                            for b in range(4, NB):
                                sample_update(t, h, b)
                        if s == 4 * h + 13:
                            dve.wait_ge(yhi_made, nth(t, 8, Y_ORDER.index(h)))
                            dve.tensor_tensor(ylo[h][:], og[h % 2][:], yhi[h][:].bitcast(F32),
                                              ALU.subtract).then_inc(ylo_made, 1)
                    if s % 4 == 0 and 12 <= s <= 24:
                        h = s // 4 - 3
                        dve.wait_ge(b5_read, b5_done(t, "o", h))
                        dve.wait_ge(rst_made, nth(t, H, h))
                        dve.tensor_tensor(og[h % 2][:], o_sb[:], rst[:], ALU.mult).then_inc(t1_made, 1)
                        dve.wait_ge(t1_made, nth(t, H, h))
                        dve.tensor_tensor(og[h % 2][:], og[h % 2][:], ga[h % 3][:], ALU.mult).then_inc(og_made, 1)
                    for g in range(G):
                        if s == 18 + 2 * g:
                            gated(t, "b", g, bg[g % 3], sb_made, cst[:, C_PS + g:C_PS + g + 1])
                        if s == 18 + 2 * g:
                            means(t, last, g)
                    if s == 21:
                        dve.wait_ge(wph_made, t + 1)
                        dve.tensor_tensor(wplo[:], wpl[:], wph[:].bitcast(F32), ALU.subtract).then_inc(wplo_made, 1)
                    if s in MEANS_SPLIT:
                        g = MEANS_SPLIT[s]
                        dve.wait_ge(pmh_made, nth(t, G, g))
                        dve.tensor_tensor(pooled_lo[g % 2][:], pooled[g % 2][:], pooled_hi[g % 2][:].bitcast(F32),
                                          ALU.subtract).then_inc(pml_made, 1)
                    if s in MIX_SLOT:
                        g = MIX_SLOT[s]
                        dve.wait_ge(mix_done, nth(t, G, g))
                        dve.wait_ge(z_sem("b", g), z_done(t, "b", g))
                        dve.tensor_tensor(bg[g % 3][:], (B6, B7)[g % 2][:, 0:T], bg[g % 3][:],
                                          ALU.mult).then_inc(ybm_made, 1)
                        dve.wait_ge(yhi_made, nth(t, 8, Y_ORDER.index(4 + g)))
                        dve.tensor_tensor(ylo[4 + g][:], bg[g % 3][:], yhi[4 + g][:].bitcast(F32),
                                          ALU.subtract).then_inc(ylo_made, 1)
                    if kind == "y":
                        merged_rest(t, j)
                    if kind == "out":
                        residual(t, j)
                        if last and 2 <= j < 2 + POOL_OUT:
                            dve.wait_ge(ysq_made, nth(t, KD, j - 2))
                            dve.tensor_scalar(xres[:, j - 2, :], xres[:, j - 2, :], cst[:, C_FG + j - 2:C_FG + j - 1],
                                              None, ALU.mult).then_inc(gained, 1)
                    if s in H_SLOT and not last:
                        h_block(t + 2, H_SLOT[s])
                        if H_SLOT[s] == KD - 1:
                            h_block(t + 2, KD)
                    if s == 27 and not last:
                        for g in range(G):
                            ins = dve.memset(rc[:, g, :], 1.0 / WINDOWS[g])
                        ins.then_inc(rc_used, 1)
                if last:
                    y_split(t, True)
                    residual(t, KD - 1)
                    output(t, range(POOL_OUT, KD))

            def y_split(t, last):
                dve.wait_ge(yacc_made, nth(t, KD - 1, KD - 3 if last else KD - 2))
                if last:
                    dve.wait_ge(ssq_done, nth(t, H, H - 1))
                else:
                    dve.wait_ge(xssq_done, t + 2)
                split_squares(yacc, "y", (ysplit_hi, ysplit), t + 1)

            def split_squares(src, what, made, value):
                dve.tensor_copy(sqh[:], src[:]).then_inc(made[0], 1)
                dve.wait_ge(made[0], value)
                dve.tensor_tensor(sql[what][:], src[:], sqh[:].bitcast(F32), ALU.subtract).then_inc(made[1], 1)

            def output(t, blocks):
                dve.wait_ge(yrs_made, t + 1)
                for j in blocks:
                    dve.scalar_tensor_tensor(out=xres[:, j, :], in0=xres[:, j, :],
                                             scalar=cst[:, C_FG + j:C_FG + j + 1], in1=yrs[:], op0=ALU.mult,
                                             op1=ALU.mult).then_inc(y_made, 1)

            zero = [ext[:, :, 0:BUF], carry[:], at_sb[:], ats[:], dprev[:]]
            for z in zero:
                dve.memset(z, 0.0).then_inc(zeroed, 1)
            dve.memset(eps_t[:], EPS).then_inc(zeroed, 1)
            dve.wait_ge(masks, 1)
            dve.tensor_copy(ones_r[:], ones[:]).then_inc(zeroed, 1)

            l0, l1 = cst[:, C_LB:C_LB + H], cst[:, C_LB + H:C_LB + 2 * H]
            dve.wait_ge(cst_landed, 16)
            dve.tensor_tensor(lb[:, 5], l0, l1, ALU.max).then_inc(lb_made, 1)
            dve.wait_ge(lb_made, 1)
            dve.tensor_tensor(lb[:, 3], l0, lb[:, 5], ALU.subtract).then_inc(lb_made, 1)
            dve.tensor_tensor(lb[:, 4], l1, lb[:, 5], ALU.subtract).then_inc(lb_made, 1)
            for k in range(2, KD):
                dve.wait_ge(xsq_made, k + 1)
                if k > 3:
                    dve.wait_ge(x0_summed, k - 3)
                dve.tensor_tensor(h0[k % 2][:], h0[k % 2][:], h0[k][:], ALU.add).then_inc(x0_summed, 1)
            dve.wait_ge(lbe_made, 1)
            dve.tensor_tensor(lb[:, 6], lb[:, 3], lb[:, 4], ALU.add).then_inc(lb_made, 1)
            dve.wait_ge(lb_made, 4)
            dve.reciprocal(lb[:, 7], lb[:, 6]).then_inc(lb_made, 1)
            dve.wait_ge(lb_made, 5)
            dve.tensor_tensor(lb[:, 0], lb[:, 3], lb[:, 7], ALU.mult).then_inc(lb_made, 1)
            dve.wait_ge(lb_made, 6)
            dve.tensor_scalar(lb[:, 1], lb[:, 0], -1.0, 1.0, ALU.mult, ALU.add).then_inc(lb_made, 1)
            dve.wait_ge(lb_made, 7)
            dve.tensor_scalar(lb[:, 2], lb[:, 1], -1.0, None, ALU.mult).then_inc(lb_made, 1)
            split(0, 0)
            dve.wait_ge(masks, MASKS)
            for g in range(G):
                dve.tensor_scalar(rc[:, g, :], rc[:, g, :], float(WINDOWS[g]), None, ALU.min).then_inc(rc_used, 1)
            dve.wait_ge(rc_used, G)
            dve.reciprocal(rc[:], rc[:]).then_inc(rc_used, 1)
            dve.wait_ge(xrs_made, 1)
            for k in range(KD):
                dve.scalar_tensor_tensor(out=h0[k][:], in0=xin[:, k, :], scalar=cst[:, C_NG + k:C_NG + k + 1],
                                         in1=xrs[:], op0=ALU.mult, op1=ALU.mult).then_inc(h32_made, 1)
            split(0, 1)
            for k in range(KD):
                dve.wait_ge(hhi_made, k + 1)
                dve.tensor_tensor(hlo[k][:], h0[k][:], hhi[k][:].bitcast(F32), ALU.subtract).then_inc(hlo_made, 1)
            for n in range(2, AHEAD):
                split(0, n)
            dve.wait_ge(lb_made, LB_STEPS)
            tile(0, False)
            with dve.Fori(1, TILES - 1) as t:
                tile(t, False)
            tile(TILES - 1, True)

        @block.gpsimd
        def _(pool):
            count = [0]

            def step(ins):
                ins.then_inc(masks, 1)
                count[0] += 1
                pool.wait_ge(masks, count[0])

            def x_sum(t, k):
                pool.wait_ge(xsq_made, (t + 1) * KD + k + 1)
                if k > 1:
                    pool.wait_ge(xacc_made, nth(t, KD - 1, k - 2))
                pool.tensor_tensor(xacc[:], xacc[:], xsq[k % 2][:], ALU.add).then_inc(xacc_made, 1)

            def y_sum(t, j):
                pool.wait_ge(ysq_made, nth(t, KD, j))
                if j > 1:
                    pool.wait_ge(yacc_made, nth(t, KD - 1, j - 2))
                pool.tensor_tensor(yacc[:], yacc[:], ysq[j % 2][:], ALU.add).then_inc(yacc_made, 1)

            def wins(level):
                return lambda lo, hi: (pa, pb)[level % 2][:, lo:hi]

            def windows(t, last, g):
                pool.wait_ge(z_sem("u", g), z_done(t, "u", g))
                if g == 0 and last:
                    pool.wait_ge(buf_landed, 16)
                if g >= 1:
                    pool.wait_ge(pooled_made, pooled_value(t, last, g - 1))
                for level in range(g + 1):
                    w = 1 << level
                    n = PT if last else T
                    if level:
                        pool.wait_ge(win_made, win_value(t, last, g, level - 1, last))
                    first = 2 * w - 1
                    if level == 0:
                        a = ext[:, g, first:BUF + n]
                        b = ext[:, g, first - w:BUF + n - w]
                    else:
                        src = wins(level - 1)
                        a, b = src(first, BUF + n), src(first - w, BUF + n - w)
                    pool.tensor_tensor(wins(level)(first, BUF + n), a, b, ALU.add).then_inc(win_made, 1)
                    if last:
                        e = BUF + NT
                        if level == 0:
                            a, b = exts[:, g, :, first:e], exts[:, g, :, first - w:e - w]
                        else:
                            ss = (pas, pbs)[(level - 1) % 2]
                            a, b = ss[:, :, first:e], ss[:, :, first - w:e - w]
                        pool.tensor_tensor((pas, pbs)[level % 2][:, :, first:e], a, b, ALU.add).then_inc(win_made, 1)

            def tile(t, last):
                for s in range(NU):
                    if s == 0 and not first(t):
                        y_sum(t - 1, KD - 1)
                    for h in range(H):
                        if s == 4 * h + 4:
                            pool.wait_ge(kin_made, nth(t, H, h))
                            pool.wait_ge(exp_made, nth(t, 4 * H, 4 * h + 2))
                            pool.tensor_tensor(e2[:], kin[h % 2][:], e2[:], ALU.mult).then_inc(k_made, 1)
                            pool.wait_ge(exp_made, nth(t, 4 * H, 4 * h + 3))
                            pool.tensor_tensor(e4[:], kin[h % 2][:], e4[:], ALU.mult).then_inc(k_made, 1)
                    for g in range(G):
                        if s == 17 + 2 * g:
                            windows(t, last, g)
                    kind, j = UNITS[s - 1] if s else (None, 0)
                    if kind == "y":
                        pool.wait_ge(z_sem("yb", j), z_done(t, "yb", j))
                        pool.wait_ge(z_sem("ya", j), z_done(t, "ya", j))
                        pool.tensor_tensor(mA[j % 2][:], mA[j % 2][:], mB[j % 2][:], ALU.add).then_inc(merged, 1)
                    if s in XSQ_SLOT and not last and XSQ_SLOT[s]:
                        x_sum(t, XSQ_SLOT[s])
                    if kind == "out" and j:
                        y_sum(t, j)
                if last:
                    pool.wait_ge(gained, POOL_OUT)
                    pool.wait_ge(yrs_made, t + 1)
                    for j in range(POOL_OUT):
                        pool.tensor_tensor(xres[:, j, :], xres[:, j, :], yrs[:], ALU.mult).then_inc(y_made_pool, 1)

            for value, m in ((1.0, ones[:]), (0.0, ident[:]), (1.0, cmask[:]), (1.0, cmask_s[:]), (1.0, bmask[:]),
                             (1.0, smask[:]), (1.0, smask_s[:]), (0.0, dfirst[:])):
                step(pool.memset(m, value))
            step(pool.affine_select(out=ident[:], in_=ident[:], compare_op=ALU.not_equal, fill=1.0, base=0,
                                    pattern=[[-1, P]], channel_multiplier=1))
            step(pool.memset(dfirst[:, :, 0:1], 1.0))
            step(pool.memset(smask[:].rearrange("p (c n) -> p c n", n=CHUNK)[:, :, 0:1], 0.0))
            step(pool.memset(smask_s[:].rearrange("p (c n) -> p c n", n=NT)[:, :, 0:1], 0.0))
            step(pool.affine_select(out=cmask[:], in_=cmask[:], compare_op=ALU.is_ge, fill=0.0, base=0,
                                    pattern=[[0, NG], [1, P]], channel_multiplier=-1))
            m = cmask_s[:]
            step(pool.affine_select(out=m, in_=m, compare_op=ALU.is_ge, fill=0.0, base=0,
                                    pattern=[[NT, NB], [1, NT]], channel_multiplier=-1))
            step(pool.affine_select(out=m, in_=m, compare_op=ALU.is_ge, fill=0.0, base=0,
                                    pattern=[[-NT, NB], [0, NT]], channel_multiplier=1))
            step(pool.affine_select(out=bmask[:], in_=bmask[:], compare_op=ALU.is_ge, fill=0.0, base=0,
                                    pattern=[[-NT, NB]], channel_multiplier=1))
            step(pool.affine_select(out=bmask[:], in_=bmask[:], compare_op=ALU.is_ge, fill=0.0, base=NT - 1,
                                    pattern=[[NT, NB]], channel_multiplier=-1))
            step(pool.iota(rc[:], pattern=[[0, G], [1, BUF]], base=1, channel_multiplier=0,
                           allow_small_or_imprecise_dtypes=True))
            assert count[0] == MASKS
            tile(0, False)
            with pool.Fori(1, TILES - 1) as t:
                tile(t, False)
            tile(TILES - 1, True)


def column_block(w, c):
    k = w.shape[0] // P
    return w[:, c:c + P].reshape(k, P, P).transpose(1, 0, 2).reshape(P, k * P)


def kernel(x_prompt, x_sample, state_hgrn, state_pool, norm_g, w_in, lb_logits, hgrn_norm_g, w_proj_a, w_pool,
           pool_scale, w_proj_b, w_out, final_norm_g):
    import concourse.bacc as bacc
    from concourse.bass_utils import run_bass_kernel_spmd

    a = [np.asarray(v) for v in (x_prompt, x_sample, state_hgrn, state_pool, norm_g, w_in, lb_logits, hgrn_norm_g,
                                 w_proj_a, w_pool, pool_scale, w_proj_b, w_out, final_norm_g)]
    (xp, xs, sh, spl, ng, win, lbl, hn, wa, wp, psc, wb, wo, fg) = a
    win, wa, wb, wo = win[0], wa[0], wb[0], wo[0]
    x = np.concatenate([xp.reshape(SEQ, D), xs.reshape(SAMPLE, D)]).reshape(TILES, T, KD, P).transpose(0, 3, 2, 1)
    width = D // 2
    first = {"q": 0, "f": width, "i": 2 * width, "g": 3 * width, "u": 4 * width, "b": 5 * width,
             "ma": 6 * width, "mb": 6 * width + D}
    blocks = []
    for kind, i in UNITS:
        if kind == "y":
            blocks.append(np.concatenate([column_block(wa, i * P), column_block(wb, i * P)], axis=1))
        elif kind == "out":
            blocks.append(column_block(wo, i * P))
        else:
            blocks.append(column_block(win, first[kind] + i * P))
    consts = np.concatenate([ng.reshape(KD, P).T, hn.reshape(1, P).T, psc.reshape(G, P).T, fg.reshape(KD, P).T,
                             lbl.reshape(2, H, P).transpose(2, 0, 1).reshape(P, 2 * H)], axis=1)
    arrays = {
        "xT": x, "w_all": np.stack(blocks), "consts": consts, "w_pool": wp[0].transpose(1, 0, 2),
        "s_in": sh[0].transpose(1, 2, 0, 3), "buf_in": spl[0].reshape(NB, BUF, G, P).transpose(3, 2, 0, 1),
    }
    arrays = {n: np.ascontiguousarray(v) for n, v in arrays.items()}
    outs = {"yT": x.shape, "sp_out": (P, H, P), "pp_out": (P, G, BUF), "ss_out": (H, P, NB, P),
            "ps_out": (P, G, NB, BUF)}
    nc = bacc.Bacc("TRN2", target_bir_lowering=False, num_devices=1)
    args = [nc.dram_tensor(n, v.shape, mybir.dt.from_np(v.dtype), kind="ExternalInput").ap()
            for n, v in arrays.items()]
    args += [nc.dram_tensor(n, v, F32, kind="ExternalOutput").ap() for n, v in outs.items()]
    step_kernel(nc, *args)
    r = run_bass_kernel_spmd(nc, [arrays], core_ids=[0]).results[0]
    y = np.asarray(r["yT"]).transpose(0, 3, 2, 1).reshape(SEQ + SAMPLE, D)
    return (
        np.ascontiguousarray(y[:SEQ]).reshape(1, SEQ, D),
        np.ascontiguousarray(y[SEQ:]).reshape(NB, NT, D),
        np.ascontiguousarray(np.asarray(r["sp_out"]).transpose(1, 0, 2)).reshape(1, 1, H, P, P),
        np.ascontiguousarray(np.asarray(r["pp_out"]).transpose(2, 1, 0)).reshape(1, 1, BUF, G * P),
        np.ascontiguousarray(np.asarray(r["ss_out"]).transpose(2, 0, 1, 3)).reshape(1, NB, H, P, P),
        np.ascontiguousarray(np.asarray(r["ps_out"]).transpose(2, 3, 1, 0)).reshape(1, NB, BUF, G * P),
    )
```
